# Optimizing a Trainium2 kernel written in Bass

```python
import jax, jax.numpy as jnp
from jax import lax
import numpy as np

D_MODEL = 1024
BATCH = 1
SEQ = 128
DEPTH = 2
DEC_BATCH = 1
DEC_SEQ = 512
PAST_LEN = 128

GRID_W = 64
N_MOD = 9
D_FF = 2816
H_MLA = 8
QK_NOPE = 64
ROPE_DIM = 32
V_HD = 64
Q_LORA = 256
KV_LORA = 128
D_MLA = H_MLA * V_HD
MLA_SCALE = (QK_NOPE + ROPE_DIM) ** -0.5
H_RWKV = 4
RWKV_HD = 64
D_RWKV = H_RWKV * RWKV_HD
LORA_WA = 64
LORA_G = 128
RWKV_COLS = 3 * D_RWKV + 4 * LORA_WA + LORA_G
DECAY_SCALE = 0.6065306597126334
RWKV_GN_EPS = 64e-5
H_RET = 4
RET_DK = 64
RET_DV = 64
D_RET = H_RET * RET_DV
RET_CHUNK = 128
RET_COLS = 2 * H_RET * RET_DK + 3 * D_RET
RET_GN_EPS = 1e-5
D_MIX = D_MLA + D_RWKV + D_RET
IN_COLS = Q_LORA + KV_LORA + ROPE_DIM + RWKV_COLS + RET_COLS
ROPE_BASE = 10000.0
Q_BLOCK = 128
NORM_EPS = 1e-6

kernel_name = 'hybrid_mla_rwkv7_retention_prefix_dit_step'

def split_cols(x, widths):
    parts, off = [], 0
    for w in widths:
        parts.append(x[..., off:off + w])
        off += w
    return parts

def rmsnorm(x, g):
    xf = x.astype(jnp.float32)
    y = xf * lax.rsqrt(jnp.mean(xf * xf, axis=-1, keepdims=True) + NORM_EPS)
    return (y * g.astype(jnp.float32)).astype(x.dtype)

def head_groupnorm(y, g, eps):
    yc = y - jnp.mean(y, axis=-1, keepdims=True)
    return yc * lax.rsqrt(jnp.mean(yc * yc, axis=-1, keepdims=True) + eps) * g

def rope_1d(x, pos):
    half = x.shape[-1] // 2
    inv = ROPE_BASE ** (-jnp.arange(half, dtype=jnp.float32) / half)
    ang = pos.astype(jnp.float32)[:, None] * inv
    cos, sin = jnp.cos(ang)[:, None, :], jnp.sin(ang)[:, None, :]
    x1, x2 = x[..., :half], x[..., half:]
    return jnp.concatenate([x1 * cos - x2 * sin, x1 * sin + x2 * cos], axis=-1)

def axial_rope(x, row, col):
    xf = x.astype(jnp.float32)
    d = x.shape[-1] // 2
    return jnp.concatenate([rope_1d(xf[..., :d], row), rope_1d(xf[..., d:], col)], axis=-1).astype(x.dtype)

def centred_shift(x, mu):
    xp = jnp.pad(x, ((0, 0), (1, 1), (0, 0)))
    return x + mu * (0.5 * (xp[:, :-2] + xp[:, 2:]) - x)

def both_dirs(t):
    return jnp.broadcast_to(t[:, None], (t.shape[0], 2) + t.shape[1:])

def to_scan_order(t):
    return jnp.concatenate([t[:, :1], jnp.flip(t[:, 1:], axis=2)], axis=1)

def swiglu(h, wi, wo):
    gu = h @ wi
    return (jax.nn.silu(gu[..., :D_FF]) * gu[..., D_FF:]) @ wo

def attend(q, k, v, scale):
    B, N, H, dk = q.shape
    nb = N // Q_BLOCK
    qb = jnp.moveaxis(q.reshape(B, nb, Q_BLOCK, H, dk), 1, 0)

    def block(qi):
        s = jnp.einsum('bqhd,bkhd->bhqk', qi, k).astype(jnp.float32) * scale
        p = jax.nn.softmax(s, axis=-1).astype(v.dtype)
        return jnp.einsum('bhqk,bkhd->bqhd', p, v)

    o = lax.map(block, qb)
    return jnp.moveaxis(o, 0, 1).reshape(B, N, H, v.shape[-1])

def mla_expand(ckv, krope_h, wkv_up):
    B, M, _ = ckv.shape
    kv = (ckv @ wkv_up).reshape(B, M, H_MLA, QK_NOPE + V_HD)
    k = jnp.concatenate([kv[..., :QK_NOPE], jnp.broadcast_to(krope_h, (B, M, H_MLA, ROPE_DIM))], axis=-1)
    return k, kv[..., QK_NOPE:]

def rwkv7_scan(r, w, kk, kka, k, v, s0):
    def step(S, inp):
        r_t, w_t, kk_t, kka_t, k_t, v_t = inp
        sa = jnp.einsum('bzhvk,bzhk->bzhv', S, -kk_t)
        S = S * w_t[..., None, :] + sa[..., None] * kka_t[..., None, :] + v_t[..., None] * k_t[..., None, :]
        return S, jnp.einsum('bzhvk,bzhk->bzhv', S, r_t)

    xs = tuple(jnp.moveaxis(t, 2, 0) for t in (r, w, kk, kka, k, v))
    s_fin, ys = lax.scan(step, s0, xs)
    return jnp.moveaxis(ys, 0, 2), s_fin

def retention_log_decay():
    e = 5.0 + jnp.arange(H_RET, dtype=jnp.float32)[None, :] + 0.5 * jnp.arange(2, dtype=jnp.float32)[:, None]
    return jnp.log1p(-jnp.exp2(-e))

def retention_chunkwise(q, k, v, s0, log_gamma):
    B, Z, N, H, dk = q.shape
    dv = v.shape[-1]
    C = RET_CHUNK
    nc = N // C
    q = q.reshape(B, Z, nc, C, H, dk)
    k = k.reshape(B, Z, nc, C, H, dk)
    v = v.reshape(B, Z, nc, C, H, dv)
    idx = jnp.arange(C, dtype=jnp.float32)
    lg = log_gamma[:, :, None]
    diff = idx[:, None] - idx[None, :]
    dmask = jnp.where(diff >= 0, jnp.exp(lg[..., None] * jnp.maximum(diff, 0.0)), 0.0)
    scores = jnp.einsum('bznihd,bznjhd->bzhnij', q, k) * dmask[None, :, :, None]
    inner = jnp.einsum('bzhnij,bznjhe->bznihe', scores, v)
    zeta = jnp.exp(lg * (C - 1.0 - idx))
    xi = jnp.exp(lg * (idx + 1.0))
    kv_chunk = jnp.einsum('bznjhd,zhj,bznjhe->nbzhde', k, zeta, v)
    g_chunk = jnp.exp(log_gamma * C)[:, :, None, None]

    def step(R, kvc):
        return R * g_chunk + kvc, R

    s_fin, r_before = lax.scan(step, s0, kv_chunk)
    cross = jnp.einsum('bznihd,zhi,nbzhde->bznihe', q, xi, r_before)
    return (inner + cross).reshape(B, Z, N, H, dv), s_fin

def token_mixer(h, lw, ctx, pos):
    B, N, _ = h.shape
    f32 = jnp.float32
    qa, kva, krope, rw, rt = split_cols(h @ lw['w_in'], [Q_LORA, KV_LORA, ROPE_DIM, RWKV_COLS, RET_COLS])

    q = (rmsnorm(qa, lw['mla_norm_q']) @ lw['mla_wq_up']).reshape(B, N, H_MLA, QK_NOPE + ROPE_DIM)
    q_nope, q_rope = q[..., :QK_NOPE], q[..., QK_NOPE:]
    ckv = rmsnorm(kva, lw['mla_norm_kv'])
    krope_h = krope[:, :, None, :]
    if pos is not None:
        q_rope = axial_rope(q_rope, pos[0], pos[1])
        krope_h = axial_rope(krope_h, pos[0], pos[1])
    k, v = mla_expand(ckv, krope_h, lw['mla_wkv_up'])
    if ctx is not None:
        kc, vc = mla_expand(ctx[0], ctx[1][:, :, None, :], lw['mla_wkv_up'])
        k = jnp.concatenate([kc, k], axis=1)
        v = jnp.concatenate([vc, v], axis=1)
    mla_o = attend(jnp.concatenate([q_nope, q_rope], axis=-1), k, v, MLA_SCALE).reshape(B, N, D_MLA)

    xr = centred_shift(rw, lw['rwkv_mu'])
    r, kr, vr, zwf, zwb, zaf, zab, zg = split_cols(xr, [D_RWKV] * 3 + [LORA_WA] * 4 + [LORA_G])
    vec = lw['rwkv_vec'].astype(f32)
    up = lw['rwkv_lora_up']
    zw = jnp.stack([jnp.tanh(zwf) @ up[0], jnp.tanh(zwb) @ up[1]], axis=1).astype(f32) + vec[None, 0:2, None]
    decay = jnp.exp(-DECAY_SCALE * jax.nn.sigmoid(zw))
    a = jax.nn.sigmoid(jnp.stack([zaf @ up[2], zab @ up[3]], axis=1).astype(f32) + vec[None, 2:4, None])
    gate = (jax.nn.sigmoid(zg) @ lw['rwkv_g_up']).astype(f32)
    r, kr, vr = r.astype(f32), kr.astype(f32), vr.astype(f32)
    kk = (kr * vec[4]).reshape(B, N, H_RWKV, RWKV_HD)
    kk = kk / (jnp.sqrt(jnp.sum(kk * kk, axis=-1, keepdims=True)) + 1e-12)
    kd = kr[:, None] * (1.0 + (a - 1.0) * vec[5])
    heads2 = lambda t: t.reshape(B, 2, N, H_RWKV, RWKV_HD)
    rh = both_dirs(r.reshape(B, N, H_RWKV, RWKV_HD))
    vh = both_dirs(vr.reshape(B, N, H_RWKV, RWKV_HD))
    kkh = both_dirs(kk)
    ah, wh, kh = heads2(a), heads2(decay), heads2(kd)
    s0 = jnp.zeros((B, 2, H_RWKV, RWKV_HD, RWKV_HD), f32) if ctx is None else ctx[2].astype(f32)
    y, s_rwkv = rwkv7_scan(to_scan_order(rh), to_scan_order(wh), to_scan_order(kkh),
                           to_scan_order(kkh * ah), to_scan_order(kh), to_scan_order(vh), s0)
    y = to_scan_order(y)
    bonus = jnp.sum(rh * kh * vec[6].reshape(H_RWKV, RWKV_HD), axis=-1, keepdims=True) * vh
    y = head_groupnorm(y, vec[7].reshape(H_RWKV, RWKV_HD), RWKV_GN_EPS) + bonus
    rwkv_o = (jnp.sum(y, axis=1).reshape(B, N, D_RWKV) * gate).astype(h.dtype)

    qr, kr2, vr2, gf, gb = split_cols(rt, [H_RET * RET_DK] * 2 + [D_RET] * 3)
    qh = qr.reshape(B, N, H_RET, RET_DK)
    kh2 = kr2.reshape(B, N, H_RET, RET_DK)
    if pos is not None:
        qh = axial_rope(qh, pos[0], pos[1])
        kh2 = axial_rope(kh2, pos[0], pos[1])
    q2 = to_scan_order(both_dirs(qh.astype(f32)))
    k2 = to_scan_order(both_dirs(kh2.astype(f32) * RET_DK ** -0.5))
    v2 = to_scan_order(both_dirs(vr2.astype(f32).reshape(B, N, H_RET, RET_DV)))
    s0r = jnp.zeros((B, 2, H_RET, RET_DK, RET_DV), f32) if ctx is None else ctx[3].astype(f32)
    o, s_ret = retention_chunkwise(q2, k2, v2, s0r, retention_log_decay())
    o = head_groupnorm(to_scan_order(o), lw['ret_gn'].astype(f32).reshape(1, 2, 1, H_RET, RET_DV), RET_GN_EPS)
    g2 = jax.nn.silu(jnp.stack([gf, gb], axis=1).astype(f32)).reshape(B, 2, N, H_RET, RET_DV)
    ret_o = jnp.sum(o * g2, axis=1).reshape(B, N, D_RET).astype(h.dtype)

    mixed = jnp.concatenate([mla_o, rwkv_o, ret_o], axis=-1) @ lw['w_out']
    return mixed, (ckv, krope, s_rwkv, s_ret)

def trunk_layer(x, mod, lw, ctx, pos):
    ng = lw['norm_g']
    m = lambda i: mod[:, i][:, None, :]
    h = rmsnorm(x, ng[0]) * (1.0 + m(1)) + m(0)
    x = x + 0.5 * m(2) * rmsnorm(swiglu(h, lw['ffn_wi'][0], lw['ffn_wo'][0]), ng[1])
    h = rmsnorm(x, ng[2]) * (1.0 + m(4)) + m(3)
    mixed, ctx_out = token_mixer(h, lw, ctx, pos)
    x = x + m(5) * rmsnorm(mixed, ng[3])
    h = rmsnorm(x, ng[4]) * (1.0 + m(7)) + m(6)
    x = x + 0.5 * m(8) * rmsnorm(swiglu(h, lw['ffn_wi'][1], lw['ffn_wo'][1]), ng[5])
    return x, ctx_out

def setup_inputs(seed: int = 0) -> dict:
    key = jax.random.key(seed)
    keys = jax.random.split(key, 40)
    counter = [0]

    def nk():
        kk = keys[counter[0]]
        counter[0] += 1
        return kk

    def nrm(shape, s=1.0):
        return s * jax.random.normal(nk(), shape, jnp.float32)

    def gain(shape):
        return 1.0 + nrm(shape, 0.05)

    rwkv_off = jnp.array([0.0, 0.0, 0.0, 0.0, 0.85, 1.0, 0.0, 1.0], jnp.float32)[None, :, None]
    rwkv_sc = jnp.array([0.5, 0.5, 0.5, 0.5, 0.05, 0.05, 0.1, 0.05], jnp.float32)[None, :, None]
    return {
        'x_prompt': nrm((BATCH, SEQ, D_MODEL)),
        'x_sample': nrm((DEC_BATCH, DEC_SEQ, D_MODEL)),
        'cache_mla_ckv': nrm((DEC_BATCH, DEPTH, PAST_LEN, KV_LORA)),
        'cache_mla_krope': nrm((DEC_BATCH, DEPTH, PAST_LEN, ROPE_DIM)),
        'state_rwkv': nrm((DEC_BATCH, DEPTH, 2, H_RWKV, RWKV_HD, RWKV_HD), 0.5),
        'state_ret': nrm((DEC_BATCH, DEPTH, 2, H_RET, RET_DK, RET_DV), 0.5),
        'c': nrm((DEC_BATCH, D_MODEL)),
        'c_ctx': nrm((D_MODEL,)),
        'norm_g': gain((DEPTH, 6, D_MODEL)),
        'w_mod': nrm((DEPTH, D_MODEL, N_MOD * D_MODEL), D_MODEL ** -0.5),
        'b_mod': nrm((DEPTH, N_MOD * D_MODEL), 0.02),
        'ffn_wi': nrm((DEPTH, 2, D_MODEL, 2 * D_FF), D_MODEL ** -0.5),
        'ffn_wo': nrm((DEPTH, 2, D_FF, D_MODEL), D_FF ** -0.5),
        'w_in': nrm((DEPTH, D_MODEL, IN_COLS), D_MODEL ** -0.5),
        'w_out': nrm((DEPTH, D_MIX, D_MODEL), D_MIX ** -0.5),
        'mla_norm_q': gain((DEPTH, Q_LORA)),
        'mla_norm_kv': gain((DEPTH, KV_LORA)),
        'mla_wq_up': nrm((DEPTH, Q_LORA, H_MLA * (QK_NOPE + ROPE_DIM)), Q_LORA ** -0.5),
        'mla_wkv_up': nrm((DEPTH, KV_LORA, H_MLA * (QK_NOPE + V_HD)), KV_LORA ** -0.5),
        'rwkv_mu': jax.random.uniform(nk(), (DEPTH, RWKV_COLS), jnp.float32),
        'rwkv_vec': rwkv_off + rwkv_sc * nrm((DEPTH, 8, D_RWKV)),
        'rwkv_lora_up': nrm((DEPTH, 4, LORA_WA, D_RWKV), 0.5 * LORA_WA ** -0.5),
        'rwkv_g_up': nrm((DEPTH, LORA_G, D_RWKV), LORA_G ** -0.5),
        'ret_gn': gain((DEPTH, 2, D_RET)),
    }

def reference(x_prompt, x_sample, cache_mla_ckv, cache_mla_krope, state_rwkv, state_ret, c, c_ctx,
              norm_g, w_mod, b_mod, ffn_wi, ffn_wo, w_in, w_out, mla_norm_q, mla_norm_kv, mla_wq_up,
              mla_wkv_up, rwkv_mu, rwkv_vec, rwkv_lora_up, rwkv_g_up, ret_gn):
    n_lat = x_sample.shape[1]
    ROWS = n_lat // GRID_W
    row = jnp.repeat(jnp.arange(ROWS), GRID_W)
    col = jnp.tile(jnp.arange(GRID_W), ROWS)
    silu_ctx = jax.nn.silu(c_ctx)[None, :]
    silu_c = jax.nn.silu(c)
    yp, ys = x_prompt, x_sample
    ckv_l, krope_l, rwkv_l, ret_l = [], [], [], []
    for l in range(DEPTH):
        lw = {'norm_g': norm_g[l], 'ffn_wi': ffn_wi[l], 'ffn_wo': ffn_wo[l], 'w_in': w_in[l],
              'w_out': w_out[l], 'mla_norm_q': mla_norm_q[l], 'mla_norm_kv': mla_norm_kv[l],
              'mla_wq_up': mla_wq_up[l], 'mla_wkv_up': mla_wkv_up[l], 'rwkv_mu': rwkv_mu[l],
              'rwkv_vec': rwkv_vec[l], 'rwkv_lora_up': rwkv_lora_up[l], 'rwkv_g_up': rwkv_g_up[l],
              'ret_gn': ret_gn[l]}
        mod_ctx = (silu_ctx @ w_mod[l] + b_mod[l]).reshape(1, N_MOD, D_MODEL)
        mod_lat = (silu_c @ w_mod[l] + b_mod[l]).reshape(-1, N_MOD, D_MODEL)
        yp, (ckv, krope, s_rwkv, s_ret) = trunk_layer(yp, mod_ctx, lw, None, None)
        ckv_l.append(ckv)
        krope_l.append(krope)
        rwkv_l.append(s_rwkv.astype(x_prompt.dtype))
        ret_l.append(s_ret.astype(x_prompt.dtype))
        ctx = (cache_mla_ckv[:, l], cache_mla_krope[:, l], state_rwkv[:, l], state_ret[:, l])
        ys, _ = trunk_layer(ys, mod_lat, lw, ctx, (row, col))
    new_mla_ckv = jnp.stack(ckv_l, axis=1)
    new_mla_krope = jnp.stack(krope_l, axis=1)
    new_rwkv = jnp.stack(rwkv_l, axis=1)
    new_ret = jnp.stack(ret_l, axis=1)
    return (yp, ys, new_mla_ckv, new_mla_krope, new_rwkv, new_ret)


_drawn_inputs = setup_inputs


def setup_inputs(seed=0):
    import zlib

    import numpy as np

    out = dict(_drawn_inputs(seed))
    spreads = {}
    factors = {'cache_mla_ckv': 2.959, 'cache_mla_krope': 5.228, 'state_rwkv': 12.058, 'mla_norm_q': 8.0}
    for name, (base, spread) in spreads.items():
        noise = np.random.default_rng([zlib.crc32(name.encode()), seed]).standard_normal(out[name].shape)
        drawn = base * np.exp(spread * noise) if base else spread * noise
        out[name] = __import__('jax').numpy.asarray(drawn.astype(out[name].dtype))
    for name, factor in factors.items():
        out[name] = (out[name] * factor).astype(out[name].dtype)
    return out
```

```python
from contextlib import ExitStack

import numpy as np

import concourse.bass as bass
from concourse import mybir

F32 = mybir.dt.float32
F32R = mybir.dt.float32r
ALU = mybir.AluOpType
ACT = mybir.ActivationFunctionType
AX = mybir.AxisListType.X

P = 128
D = 1024
KD = D // P
DEPTH = 2
LAT, CTX, PAST = 512, 128, 128
TOK = LAT + CTX
NT = TOK // P
NL = LAT // P
D_FF = 2816
NF = D_FF // P
H_MLA, NOPE, ROPE, VHD = 8, 64, 32, 64
QL, KVL = 256, 128
NH, HD = 4, 64
DR = NH * HD
DECAY_SCALE = 0.6065306597126334
NORM_EPS, RWKV_EPS, RET_EPS = 1e-6, 64e-5, 1e-5
MLA_SCALE = (NOPE + ROPE) ** -0.5
NMOD = 9
UNITS = {"ffn": NF, "mix": 12}
OUT_UNITS = {"ffn": NF // 2, "mix": KD // 2}
MOD_UNIT = 4
SUBS = ("ffn", "mix", "ffn")
MOD_FIRST = 6
MOD_UNITS = DEPTH * NMOD * KD // MOD_UNIT


def mod_share(l, s):
    per = NMOD * KD // MOD_UNIT
    if s == 0:
        return l * per + MOD_FIRST, 10
    return (l * per + 16, 8) if l + 1 < DEPTH else (l * per + 16, 2)


RW_R, RW_K, RW_V, RW_ZW, RW_ZA, RW_ZG = 0, 2, 4, 6, 7, 8
NRW = 9
RWW = 644


def rw_col(t):
    return 1 + P * t if t < NL else 2 + LAT


C_GQ, C_GKV, C_MU, C_V4, C_V5, C_V6, C_AB, C_N = 0, 2, 3, 12, 14, 16, 18, 22
SHIFT_AT = {7: (0, 1), 8: (2, 3), 9: (4, 5), 10: (6, 7), 11: (8,)}


class Fixed:

    def __init__(self, start, size):
        self.at, self.end = start, start + size

    def take(self, words):
        start = self.at
        self.at += (4 * words + 31) // 32 * 32
        assert self.at <= self.end, (self.at, self.end)
        return start


def build(nc, i, o):
    ctx = ExitStack()
    with ctx:
        base = (nc.sbuf_base + 127) // 128 * 128
        whole = Fixed(base, nc.sbuf_usable_end - base)

        def place(name, shape, at, dt=F32):
            return nc.alloc_sbuf_tensor_at(name, shape, dt, offset=at)

        def words(shape):
            return int(np.prod(shape[1:]))

        def keep(name, shape, region=whole, dt=F32):
            return place(name, shape, region.take(words(shape)), dt)

        x = keep("x", [P, NT, D])
        ident = keep("ident", [P, P])
        ones = keep("ones", [P, P])
        csil = keep("csil", [P, KD, 2])
        modc = keep("modc", [P, DEPTH * NMOD * KD, 2])
        bmod = keep("bmod", [P, DEPTH * NMOD * KD])
        ngc = keep("ngc", [P, DEPTH * 6, KD])
        affA = keep("affA", [P, KD, 2])
        gcol = keep("gcol", [P, KD, 2])
        stat = keep("stat", [P, 5, NT])
        powe = keep("powe", [P, 8])
        gates = keep("gates", [P, 2, D])
        sg = keep("sg", [P, 2, TOK])
        macc = keep("macc", [P, 2, MOD_UNIT * P])
        r_wor = whole.take(2 * 2 * 512)
        r_mod = whole.take(KD * MOD_UNIT * P)
        r_act = whole.take(NF * TOK)
        r_big = whole.take(2 * KD * TOK + 6 * KD * 256)
        act = place("act", [P, NF, TOK], r_act)
        h_hi = place("h_hi", [P, KD, TOK], r_big, F32R)
        h_lo = place("h_lo", [P, KD, TOK], r_big + 4 * KD * TOK, F32R)
        r_wi = r_big + 8 * KD * TOK
        wi = place("wi", [P, 2, KD, 256], r_wi)
        wi_hi = place("wi_hi", [P, 2, KD, 256], r_wi + 8 * KD * 256, F32R)
        wi_lo = place("wi_lo", [P, 2, KD, 256], r_wi + 16 * KD * 256, F32R)
        wm = place("wm", [P, KD, MOD_UNIT * P], r_mod)
        mprod = place("mprod", [P, 2, MOD_UNIT * P], r_wor)
        wo = place("wo", [P, 2, 2, 512], r_wor)
        wo_hi = place("wo_hi", [P, 2, 2, 512], r_mod, F32R)
        wo_lo = place("wo_lo", [P, 2, 2, 512], r_mod + 4 * 2 * 2 * 512, F32R)
        y = place("y", [P, NT, D], r_big)
        a_hi = place("a_hi", [P, 2, 2, TOK], r_big + 4 * NT * D, F32R)
        a_lo = place("a_lo", [P, 2, 2, TOK], r_big + 4 * NT * D + 16 * TOK, F32R)
        pre = Fixed(r_act, 4 * NF * TOK)
        xn = keep("xn", [P, 2, D], pre)
        h32 = keep("h32", [P, 2, KD, P], pre)
        junk = keep("junk", [P, D], pre)
        diag = keep("diag", [P, 2, 4, P], Fixed(r_wi, 8192))
        wm0 = [place(f"wm0_{n}", [P, KD, MOD_UNIT * P], at) for n, at in enumerate(
            [r_act, r_act + 16384, r_act + 32768, r_big, r_big + 16384, r_mod])]
        PS = ctx.enter_context(nc.psum_tensor("PS", [P, 8, 512], F32))
        PSF = PS[:, :, :].rearrange("p b n -> p (b n)")

        def sem(name):
            return ctx.enter_context(nc.semaphore(name))

        s_const = sem("const_loaded")
        s_x0 = sem("x_loaded")
        s_c = sem("c_silu")
        s_one = sem("constants_set")
        s_w0 = [sem(f"mod0_loaded{n}") for n in range(MOD_FIRST)]
        s_wm = sem("mod_loaded")
        s_ma = [sem(f"mod_sum_stream{z}") for z in range(2)]
        s_mp = sem("mod_products")
        s_mm = sem("mod_multiplied")
        s_me = sem("mod_written")
        s_aff = sem("affine_ready")
        s_gc = sem("gate_columns")
        s_sq = sem("x_squared")
        s_rms = sem("x_meansq")
        s_rs = sem("x_rstd")
        s_xn = sem("x_normed")
        s_xT = sem("x_transposed")
        s_hA = sem("h_lower_half")
        s_hD = sem("h_upper_half")
        s_hhi = sem("h_hi")
        s_hlo = sem("h_lo_even_tiles")
        s_hlp = sem("h_lo_odd_tiles")
        s_wi = [sem(f"wi_loaded{n}") for n in range(2)]
        s_wih = sem("wi_hi")
        s_wil = sem("wi_lo")
        s_in = sem("in_multiplied")
        s_ea = sem("in_first_half_out")
        s_eb = sem("in_second_half_out")
        s_g = sem("gate_diag")
        s_gm = sem("gate_rows")
        s_ge = sem("gate_rows_out")
        s_wo = [sem(f"wo_loaded{n}") for n in range(2)]
        s_oh = sem("out_hi")
        s_ol = sem("out_lo")
        s_om = sem("out_multiplied")
        s_y = sem("y_half_out")
        s_ysq = sem("y_squared")
        s_yms = sem("y_meansq")
        s_yrs = sem("y_rstd")
        s_x = sem("x_updated")
        s_store = sem("stored")

        UPL = sum(UNITS[s] for s in SUBS)
        VPL = sum(2 * OUT_UNITS[s] for s in SUBS)

        def u0(n):
            l, s = divmod(n, 3)
            return l * UPL + sum(UNITS[SUBS[q]] for q in range(s))

        def v0(n):
            l, s = divmod(n, 3)
            return l * VPL + sum(2 * OUT_UNITS[SUBS[q]] for q in range(s))

        def m0(n):
            l, s = divmod(n, 3)
            return [mod_share(l, 0)[0], mod_share(l, 0)[0] + 10, mod_share(l, 2)[0]][s]

        def ffn_parts(n):
            m = mod_share(n // 3, n % 3)[1]
            runs = [(0, 1, True), (1, m, True), (m, m + 1, False), (m + 1, NF // 2, False)]
            return [r for r in runs if r[1] > r[0]]

        def pair_runs(n, half):
            m = (OUT_UNITS[SUBS[n % 3]] - 1) // 2
            return [(0, 1), (1, m)] if n == 0 and half == 0 else [(0, m)]

        def over(eng, a, b, body):
            if b - a == 1:
                body(a)
                return
            with eng.Fori(a, b) as step:
                body(step)

        def tile_at(t3, n):
            return t3[:, bass.ds(n, 1), :].rearrange("p a n -> p (a n)")

        def low_part_done(eng, n, t):
            if t % 2:
                eng.wait_ge(s_hlp, (NT // 2) * n + t // 2 + 1)
            else:
                eng.wait_ge(s_hlo, (NT - NT // 2) * n + t // 2 + 1)

        SUBN = range(3 * DEPTH)

        class Stage:

            def __init__(self, sem, per, turn=0, turns=1):
                self.sem, self.per, self.turn, self.turns = sem, per, turn, turns

            def value(self, l, k):
                return self.turns * (self.per * l + k - 1) + self.turn + 1

        mcol = keep("mcol", [P, C_N])
        mcon = keep("mcon", [P, 2, NRW])
        sml = keep("sml", [P, 40])
        half = keep("half", [P, 8])
        ra = Fixed(r_act, 4 * NF * TOK)
        rwz = keep("rwz", [P, NRW, RWW], ra)
        at_mz = ra.at
        mz = keep("mz", [P, 4, TOK], ra)
        mla_o = place("mla_o", [P, NT, 512], at_mz)
        at_rqk = ra.at
        rqk = keep("rqk", [P, 4, TOK], ra)
        retv = keep("retv", [P, NT, DR], ra)
        rm = Fixed(r_mod, 4 * 4096)
        gts = keep("gts", [P, NT, 512], rm)
        at_free2 = rm.at
        ro = Fixed(r_wor, 8192)
        cosm = keep("cosm", [P, TOK], ro)
        sinm = keep("sinm", [P, TOK], ro)
        wk = keep("wk", [P, 512], rm)
        wv = keep("wv", [P, 512], rm)
        rb = Fixed(r_big, 4 * 22528)
        QT = keep("QT", [P, H_MLA, TOK], rb)
        KT = keep("KT", [P, H_MLA, PAST + TOK], rb)
        V = keep("V", [P, 6, 512], rb)
        at_p = rb.at
        Pm = keep("Pm", [P, 2, TOK], rb)
        PT = keep("PT", [P, 2, TOK], rb)
        sqt = place("sqt", [P, 3, TOK], at_p)
        at_tab = rb.at
        wq = keep("wq", [P, 2, 1024], rb)
        ckvT = keep("ckvT", [P, PAST + TOK], rb)
        krT = keep("krT", [P, PAST + TOK], rb)
        rtmp = keep("rtmp", [P, TOK], rb)
        co = keep("co", [P, 160], rb)
        mx = keep("mx", [P, 40], rb)
        nb = keep("nb", [P, 40], rb)
        rsum = keep("rsum", [P, 40], rb)
        rinv = keep("rinv", [P, 40], rb)
        ro = Fixed(r_wor, 8192)
        cosr = keep("cosr", [P, TOK], ro)
        sinr = keep("sinr", [P, TOK], ro)
        rb = Fixed(r_big, 4 * 22528)
        rt = Fixed(at_tab, 4 * 4224)
        permT = keep("permT", [P, P], rt)
        dmask = keep("dmask", [P, NH, 2, P], rt)
        xi = keep("xi", [P, 2, 2, P], rt)
        zeta = keep("zeta", [P, NH, 2], rt)
        gch = keep("gch", [P, 2, 2], rt)
        rgn = keep("rgn", [P, 512], rt)
        Rall = keep("Rall", [P, NL, 2, 2, HD], rt)
        rot = keep("rot", [P, 2, TOK], rb)
        ktok = keep("ktok", [P, NT, DR], rb)
        vz = keep("vz", [P, 2, NH, 2, HD], rb)
        kvs = keep("kvs", [P, NT, 2, 2, HD], rb)
        Sm = keep("Sm", [P, 2, NH, 2, P], rb)
        qxi = keep("qxi", [P, 2, 2, 2, P], rb)
        yc = keep("yc", [P, 2, 512], rb)
        sqg = keep("sqg", [P, 2, 512], rb)
        gs = keep("gs", [P, 2, 512], rb)
        gst = keep("gst", [P, 2, 4, 8], rb)
        rb = Fixed(r_big, 4 * 22528)
        kk = keep("kk", [P, 2, RWW], rb)
        MTs = keep("MTs", [P, NL, 2, 2, HD], rb)
        Ns = keep("Ns", [P, NT, 2, 2, HD], rb)
        RGs = keep("RGs", [P, NL, 2, 2, P], rb)
        Yls = keep("Yls", [P, NT, 512], rb)
        PCs = keep("PCs", [P, NT, 2, 2], rb)
        bv = keep("bv", [P, NT, DR], rb)
        STa = keep("STa", [P, NL, 2, 2, HD], rb)
        at_ch = rb.at
        LB = [keep(f"LB{d}", [P, NH, 2, P], rb) for d in range(2)]
        LK = [keep(f"LK{d}", [P, NH, 2, P], rb) for d in range(2)]
        sgw = keep("sgw", [P, 512], rb)
        Pinv = keep("Pinv", [P, 2, 2, P], rb)
        ab = keep("ab", [P, 2, 2, P], rb)
        kd = keep("kd", [P, 2, 2, P], rb)
        rk = keep("rk", [P, 2, P], rb)
        LM = [keep(f"LM{d}", [P, NH, P], rb) for d in range(2)]
        R = [[keep(f"R{s}_{d}", [P, NH, P], rb) for d in range(2)] for s in range(2)]
        rq = Fixed(at_rqk, 4 * 4 * TOK)
        XT = [keep(f"XT{d}", [P, NH, P], rq) for d in range(2)]
        X = [keep(f"X{d}", [P, NH, P], rq) for d in range(2)]
        vtok = keep("vtok", [P, 2, DR], rq)
        fo = Fixed(r_wor, 8192)
        T1 = [keep(f"T1_{d}", [P, NH, P], fo) for d in range(2)]
        upw = keep("upw", [P, DR], fo)
        upa = keep("upa", [P, DR], fo)
        gup = keep("gup", [P, DR], fo)
        v7 = keep("v7", [P, DR], fo)
        f2 = Fixed(r_mod, 4 * 4096)
        E = [keep(f"E{s}", [P, 2, 2, 2, P], f2) for s in range(2)]
        btok = keep("btok", [P, 2, 2, DR], f2)
        tri = keep("tri", [P, 2, 256], f2)
        mask2 = keep("mask2", [P, 2, 2, P], f2)
        fa = Fixed(ra.at, r_act + 4 * NF * TOK - ra.at)
        lvl = keep("lvl", [P, 2, 7, P], fa)
        kptok = keep("kptok", [P, 2, 2, DR], rb)
        v01 = keep("v01", [P, 512], rb)
        blk = keep("blk", [P, P], rb)
        hsel = keep("hsel", [P, 2], rb)
        id64 = keep("id64", [P, HD], rb)
        ssh = place("ssh", [P, 2, RWW], ra.at)
        ksq = place("ksq", [P, 2, RWW], at_ch)
        knorm = place("knorm", [P, 2, RWW], at_ch + 4 * 2 * RWW)
        yc2 = place("yc2", [P, 2, 512], at_ch)
        sqg2 = place("sqg2", [P, 2, 512], at_ch + 4096)
        gst2 = place("gst2", [P, 2, 4, 8], at_ch + 8192)
        rsumd = place("rsumd", [P, 2, DR], at_ch + 8192 + 512)

        GN = ((yc, sqg, gst), (yc2, sqg2, gst2))
        S = {}

        def stage(name, per):
            S[name] = Stage(ctx.enter_context(nc.semaphore(name)), per)

        def series(name, per, *names):
            s_ = ctx.enter_context(nc.semaphore(name))
            for turn, one in enumerate(names):
                S[one] = Stage(s_, per, turn, len(names))

        stage("mix_columns", 16)
        stage("mla_tables", 16 * 4)
        stage("mla_weights", 16 * 3)
        stage("ret_tables", 16 * 10)
        stage("rwkv_tables", 16 * 11)
        stage("rwkv_states", 16 * 2)
        stage("mix_stored", 16 * 4)
        for name, per in (("sq_qkv", 1), ("ss_qkv", 2), ("q_gained", 1), ("ms_q", 1), ("rs_q", 3), ("ms_kv", 1),
                          ("rt_kv", 1), ("rc_kv", 1), ("ckv", 1), ("kr", 3), ("kr_all", 1), ("q_mm", 8), ("q_top", 8),
                          ("q_rope", 24), ("co_T", 1), ("co", 1), ("k_mm", 4), ("k_even", 4), ("k_odd", 4), ("v_mm", 6),
                          ("v_out", 6), ("s_mm", 40), ("s_max", 40), ("s_bias", 40), ("p_exp", 40), ("p_T", 40),
                          ("pt_a", 40), ("pt_b", 32), ("pv", 40), ("r_inv", 5), ("o_out", 5)):
            stage(name, per)
        for name, per in (("rot_mm", 4), ("rot_sin", 4), ("rot_cos", 4), ("roped", 4), ("kt_T", 5), ("kt_out", 5),
                          ("v_decayed", 5), ("kv_mm", 5), ("kv_out", 5), ("ret_chain", 12), ("rs_mm", 5), ("rs_masked", 5),
                          ("q_decayed", 4), ("ro_mm", 5), ("ret_in", 2)):
            stage(name, per)
        for name, per in (("gn_sq", 10), ("gn_scaled", 10), ("g_silu", 5), ("g_gain", 5), ("g_mul", 5), ("ret_o", 5)):
            stage(name, per)
        series("gn_statistics", 10, "gn_sum", "gn_mean", "gn_centred", "gn_ss")
        series("gn_rstd", 10, "gn_ms", "gn_rs")
        for name, per in (("mu_cols", 4), ("pads", 1), ("nbr_sum", 9), ("own_part", 9), ("shifted", 9), ("kk_gain", 2),
                          ("kk_sq", 1), ("kk_ss", 1), ("kk_rt", 1), ("kk_inv", 2), ("kk", 1), ("lora_act", 2),
                          ("zg_sig", 1)):
            stage(name, per)
        series("chunk_tensor", 5, "wa_mm", "cs_mm", "tok_T")
        series("chunk_scalar", 5, "w_tanh", "a_tanh", "decays", "p_inv", "alpha_tok", "kappa_tok")
        series("chunk_vector", 5, "w_bias", "w_sig", "a_sig", "pc", "alpha", "rho", "b_a", "beta", "rk", "beta_tok", "v_tok",
               "bv")
        series("chunk_gpsimd", 5, "kd_a", "kd", "kd_sum", "kappa")
        series("solve_products", 5, "lb_mm0", "lb_mm1", "lk_mm0", "lk_mm1", "lm_T0", "lm_T1", "lv_mm0", "lv_mm1")
        series("masked_products", 5, "lb0", "lb1", "lk0", "lk1")
        series("lak_v", 5, "lv0", "lv1")
        series("level_lx", 30, "t1_mm0", "t1_mm1")
        series("level_lx_out", 30, "t10", "t11")
        series("solve_results", 5, "gh_mm0", "gh_mm1", "fin_mm0", "yl_mm0", "fin_mm1", "yl_mm1")
        series("gh_out", 5, "gh0", "gh1")
        series("yl", 5, "yl_out0", "yl_out1")
        series("n", 5, "n_out0", "n_out1")
        series("mt_rg", 4, "mt_out0", "rg_out0", "mt_out1", "rg_out1")
        series("level_masks", 35, "lm0", "lm1")
        for d in range(2):
            for name, per in (("x", 30), ("xt", 35), ("dx_mm", 25), ("dxt_mm", 30)):
                stage(name + str(d), per)
        for name, per in (("st_mm", 3), ("st_out", 3), ("y_mm", 4), ("y_sum", 4), ("gate_mm", 5), ("mixT_mm", 5), ("mixT_a", 5), ("mixT_b", 5)):
            stage(name, per)
        series("rwkv_finish", 5, "y_dirs", "y_gain", "y_bonus", "rwkv_o")

        def until(eng, l, name, k):
            if S[name].per * l + k > 0:
                eng.wait_ge(S[name].sem, S[name].value(l, k))

        def PP(bank, at, n):
            return PSF[:, bank * 512 + at:bank * 512 + at + n]

        def mix_sync(sp, l):
            n = 3 * l + 1
            sp.wait_ge(s_om, v0(n))
            for dst, src in ((cosm, i["cosm"]), (sinm, i["sinm"]), (wk, i["wk"][l]),
                             (wv, i["wv"][l])):
                sp.dma_start(dst[:], src).then_inc(S["mla_tables"].sem, 16)
            sp.wait_ge(s_eb, u0(n) + UNITS["mix"])
            for dst, src in ((wq[:], i["wq"][l]), (ckvT[:, 0:PAST], i["ckvc"][l]), (krT[0:ROPE, 0:PAST], i["krc"][l])):
                sp.dma_start(dst, src).then_inc(S["mla_weights"].sem, 16)
            until(sp, l, "co", 1)
            sp.dma_start(o["ckv"][l], co[:, 0:KVL]).then_inc(S["mix_stored"].sem, 16)
            sp.dma_start(o["krope"][l], co[:, KVL:KVL + ROPE]).then_inc(S["mix_stored"].sem, 16)
            until(sp, l, "kr_all", 1)
            until(sp, l, "q_mm", 8)
            until(sp, l, "v_mm", 6)
            for dst, src in ((cosr[:], i["cosr"]), (sinr[:], i["sinr"]), (permT[:], i["permT"]), (dmask[:], i["dmask"]),
                             (xi[:], i["xi"]), (zeta[:], i["zeta"]), (gch[:], i["gch"]), (rgn[:], i["rgn"][l]),
                             (Rall[:, 0, 0, :, :], i["st_ret"][l][:, 0]), (Rall[:, NL - 1, 1, :, :], i["st_ret"][l][:, 1])):
                sp.dma_start(dst, src).then_inc(S["ret_tables"].sem, 16)
            until(sp, l, "roped", 4)
            until(sp, l, "o_out", 5)
            until(sp, l, "mix_stored", 32)
            until(sp, l, "shifted", NRW)
            for dst, src in ((tri[:], i["tri"]), (mask2[:], i["mask2"]), (v01[:], i["v01"][l]), (lvl[:], i["lvl"]),
                             (blk[:], i["blk"]), (upw[:], i["upw"][l]), (upa[:], i["upa"][l]), (gup[:], i["gup"][l]),
                             (v7[:], i["v7"][l]), (hsel[:], i["hsel"]), (id64[:], i["id64"])):
                sp.dma_start(dst, src).then_inc(S["rwkv_tables"].sem, 16)
            until(sp, l, "kv_out", 5)
            sp.dma_start(o["s_ret"][l], kvs[:, NL, :, :, :]).then_inc(S["mix_stored"].sem, 16)
            until(sp, l, "ret_o", 5)
            until(sp, l, "mix_stored", 48)
            for dst, src in ((STa[:, 0, 0, :, :], i["st_rwkv"][l][:, 0]),
                             (STa[:, NL - 1, 1, :, :], i["st_rwkv"][l][:, 1])):
                sp.dma_start(dst, src).then_inc(S["rwkv_states"].sem, 16)
            until(sp, l, "n_out0", 5)
            until(sp, l, "n_out1", 5)
            sp.dma_start(o["s_rwkv"][l], Ns[:, NL, :, :, :]).then_inc(S["mix_stored"].sem, 16)
            until(sp, l, "mix_stored", 64)
            until(sp, l, "gate_mm", 5)
            until(sp, l, "y_gain", 5)

        def split(bank, rows=P):
            return ((0, 384, PSF[0:rows, bank * 512 + P:bank * 512 + 512]),
                    (384, TOK, PSF[0:rows, bank * 512 + 512:bank * 512 + 768]))

        def mix_tensor(pe, l):
            until(pe, l, "sq_qkv", 1)
            for t in range(NT):
                for k in range(2):
                    mm = pe.matmul(PS[:, 7, t:t + 1], sqt[:, k, t * P:(t + 1) * P], ones[:, 0:1],
                                   start=(k == 0), stop=(k == 1))
            mm.then_inc(S["ss_qkv"].sem, 1)
            for a, b, dst in split(4):
                mm = pe.matmul(dst, ones[:], sqt[:, 2, a:b], start=True, stop=True)
            mm.then_inc(S["ss_qkv"].sem, 1)
            until(pe, l, "q_gained", 1)
            until(pe, l, "mla_weights", 48)
            for h in range(H_MLA):
                if h >= 2:
                    until(pe, l, "q_top", h - 1)
                    until(pe, l, "q_rope", 3 * (h - 1))
                for k in range(2):
                    for a, b, dst in split(2 * (h % 2)):
                        mm = pe.matmul(dst, wq[:, k, h * P:(h + 1) * P], mz[:, k, a:b], start=(k == 0), stop=(k == 1))
                mm.then_inc(S["q_mm"].sem, 1)
            until(pe, l, "ckv", 1)
            pe.transpose(PS[:, 7, 0:P], ckvT[:, PAST + LAT:PAST + TOK], ident[:])
            pe.transpose(PS[:, 7, P:P + ROPE], mz[0:ROPE, 3, LAT:TOK], ident[0:ROPE, 0:ROPE])\
                .then_inc(S["co_T"].sem, 1)
            for hp in range(4):
                until(pe, l, "q_top", min(7 + hp, 8))
                until(pe, l, "q_rope", min(21 + 3 * hp, 24))
                if hp >= 2:
                    until(pe, l, "k_even", hp - 1)
                    until(pe, l, "k_odd", hp - 1)
                b = 2 * (hp % 2)
                for c in range(2):
                    mm = pe.matmul(PP(b, P, 384) if c == 0 else PP(b + 1, 0, 384), wk[:, hp * P:(hp + 1) * P],
                                   ckvT[:, c * 384:(c + 1) * 384], start=True, stop=True)
                mm.then_inc(S["k_mm"].sem, 1)
            for kt in range(6):
                bank = 4 + kt % 4
                if kt == 3:
                    until(pe, l, "co", 1)
                if kt >= 4:
                    until(pe, l, "v_out", kt - 3)
                pe.matmul(PS[:, bank, :], ckvT[:, kt * P:(kt + 1) * P], wv[:], start=True, stop=True)\
                    .then_inc(S["v_mm"].sem, 1)

            def scores(x_):
                t, h = divmod(x_, H_MLA)
                if x_ >= 2:
                    until(pe, l, "p_exp", x_ - 1)
                else:
                    until(pe, l, "k_even", 4)
                    until(pe, l, "k_odd", 4)
                    until(pe, l, "kr_all", 1)
                q = QT[0:96, h, t * P:(t + 1) * P]
                b = 2 * (x_ % 2)
                if t < NL:
                    for a, z, dst in split(b):
                        mm = pe.matmul(dst, q, KT[0:96, h, a:z], start=True, stop=True)
                else:
                    mm = pe.matmul(PP(b, P, P), q, KT[0:96, h, PAST + LAT:], start=True, stop=True)
                mm.then_inc(S["s_mm"].sem, 1)

            def turn(x_):
                t = x_ // H_MLA
                until(pe, l, "p_exp", x_ + 1)
                until(pe, l, "pt_a", x_)
                until(pe, l, "pt_b", min(x_, 32))
                if x_ == 0:
                    until(pe, l, "v_out", 6)
                for kt in range(5 if t < NL else 1):
                    mm = pe.transpose(PP(4, kt * P, P), Pm[:, x_ % 2, kt * P:(kt + 1) * P], ident[:])
                mm.then_inc(S["p_T"].sem, 1)

            def values(x_):
                t, h = divmod(x_, H_MLA)
                until(pe, l, "pt_a", x_ + 1)
                until(pe, l, "pt_b", min(x_ + 1, 32))
                if t >= 2:
                    until(pe, l, "o_out", t - 1)
                nk = 5 if t < NL else 1
                for kt in range(nk):
                    mm = pe.matmul(PS[:, 6 + t % 2, h * VHD:(h + 1) * VHD], PT[:, x_ % 2, kt * P:(kt + 1) * P],
                                   V[:, kt if t < NL else 5, h * VHD:(h + 1) * VHD], start=(kt == 0), stop=(kt == nk - 1))
                mm.then_inc(S["pv"].sem, 1)

            scores(0)
            scores(1)
            for x_ in range(40):
                turn(x_)
                if x_ + 2 < 40:
                    scores(x_ + 2)
                if x_:
                    values(x_ - 1)
            values(39)

            until(pe, l, "ret_tables", 160)
            for f in range(4):
                if f < 2:
                    until(pe, l, "p_exp", 40)
                else:
                    until(pe, l, "rot_sin", f - 1)
                for a, b, dst in split(2 * (f % 2)):
                    mm = pe.matmul(dst, permT[:], rqk[:, f, a:b], start=True, stop=True)
                mm.then_inc(S["rot_mm"].sem, 1)

            def k_turn(t):
                if t >= 2:
                    until(pe, l, "kt_out", t - 1)
                for ft in range(2):
                    mm = pe.transpose(PS[:, 4 + t % 2, ft * P:(ft + 1) * P], rqk[:, 2 + ft, t * P:(t + 1) * P], ident[:])
                mm.then_inc(S["kt_T"].sem, 1)

            def kv(t):
                until(pe, l, "kt_out", t + 1)
                until(pe, l, "v_decayed", t + 1)
                if t >= 2:
                    until(pe, l, "kv_out", t - 1)
                for h in range(NH):
                    ft, pr = divmod(h, 2)
                    dst = PS[pr * HD:(pr + 1) * HD, 6 + t % 2, 0:256].rearrange("p (d f v) -> p d f v", d=2, f=2)
                    mm = pe.matmul(dst[:, :, ft, :], ktok[:, t, h * HD:(h + 1) * HD], vz[:, t % 2, h, :, :],
                                   start=True, stop=True)
                mm.then_inc(S["kv_mm"].sem, 1)

            until(pe, l, "roped", 4)
            for t in range(NT + 1):
                if t < NT:
                    k_turn(t)
                if t:
                    kv(t - 1)

            def ret_scores(t):
                if t >= 2:
                    until(pe, l, "rs_masked", t - 1)
                for h in range(NH):
                    ft, pr = divmod(h, 2)
                    r = slice(pr * HD, (pr + 1) * HD)
                    mm = pe.matmul(PS[:, t % 2 + 4 * pr, ft * P:(ft + 1) * P], rqk[r, 2 + ft, t * P:(t + 1) * P],
                                   rqk[r, ft, t * P:(t + 1) * P], start=True, stop=True)
                mm.then_inc(S["rs_mm"].sem, 1)

            def ret_out(t):
                until(pe, l, "rs_masked", t + 1)
                if t < NL:
                    until(pe, l, "q_decayed", t + 1)
                    until(pe, l, "ret_chain", 12)
                if t >= 2:
                    until(pe, l, "gn_centred", t - 1)
                for d in range(2):
                    for h in range(NH):
                        ft, pr = divmod(h, 2)
                        r = slice(pr * HD, (pr + 1) * HD)
                        dst = PS[:, 2 + pr + 4 * (t % 2), (2 * d + ft) * HD:(2 * d + ft + 1) * HD]
                        mm = pe.matmul(dst, Sm[:, t % 2, h, d, :], retv[:, t, h * HD:(h + 1) * HD], start=True,
                                       stop=(t == NL))
                        if t < NL:
                            mm = pe.matmul(dst, qxi[r, t % 2, d, ft, :], Rall[r, t, d, ft, :], start=False, stop=True)
                mm.then_inc(S["ro_mm"].sem, 1)

            for t in range(NT + 1):
                if t < NT:
                    ret_scores(t)
                if t:
                    ret_out(t - 1)
            rwkv_tensor(pe, l)

        def first_half_out(a_, l, q):
            n, j = 3 * l + 1, q % 2
            a_.wait_ge(s_in, u0(n) + q + 1)
            src = PP(3 * j, P, TOK)
            if q < 2 or q in (6, 7):
                dst = {0: mz[:, 0, :], 1: mz[:, 2, :], 6: rqk[:, 0, :], 7: rqk[:, 2, :]}[q]
                a_.activation(dst, src, ACT.Copy).then_inc(s_ea, 1)
            elif q < 8:
                f = {2: RW_R, 3: RW_K, 4: RW_V, 5: RW_ZW}[q]
                a_.activation(rwz[:, f, 1:1 + LAT], src[:, 0:LAT], ACT.Copy)
                a_.activation(rwz[:, f, 2 + LAT:2 + TOK], src[:, LAT:TOK], ACT.Copy).then_inc(s_ea, 1)
            elif q == 8:
                a_.activation(rwz[:, RW_ZG, 1:1 + 384], src[:, 0:384], ACT.Copy).then_inc(s_ea, 1)
            else:
                dst = retv if q == 11 else gts[:, :, (q - 9) * 256:(q - 8) * 256]
                a_.activation(dst[:, 0:2, :], PS[:, 3 * j, :].rearrange("p (t n) -> p t n", t=2), ACT.Copy)\
                    .then_inc(s_ea, 1)

        def mix_scalar(a_, l):
            n = 3 * l + 1
            a_.wait_ge(s_eb, u0(n) + UNITS["mix"])
            a_.activation(sqt[:], mz[:, 0:3, :], ACT.Square).then_inc(S["sq_qkv"].sem, 1)
            until(a_, l, "mla_tables", 64)
            until(a_, l, "sq_qkv", 1)
            for k in range(2):
                m = a_.activation(mz[:, k, :], mz[:, k, :], ACT.Copy, scale=mcol[:, C_GQ + k:C_GQ + k + 1])
            m.then_inc(S["q_gained"].sem, 1)
            for h in range(H_MLA):
                until(a_, l, "q_mm", h + 1)
                a_.activation(QT[0:NOPE, h, :], PSF[0:NOPE, 2 * (h % 2) * 512 + P:2 * (h % 2) * 512 + P + TOK],
                              ACT.Copy).then_inc(S["q_top"].sem, 1)
                if h == 1:
                    until(a_, l, "ms_kv", 1)
                    a_.activation(rtmp[:], rtmp[:], ACT.Sqrt).then_inc(S["rt_kv"].sem, 1)
            for hp in range(4):
                until(a_, l, "k_mm", hp + 1)
                b = 2 * (hp % 2) * 512 + P
                a_.activation(KT[0:NOPE, 2 * hp, :], PSF[0:NOPE, b:b + 768], ACT.Copy).then_inc(S["k_even"].sem, 1)
            for kt in range(6):
                until(a_, l, "v_mm", kt + 1)
                a_.activation(V[:, kt, :], PS[:, 4 + kt % 4, :], ACT.Copy).then_inc(S["v_out"].sem, 1)

            def probs(x_):
                t = x_ // H_MLA
                until(a_, l, "s_bias", x_ + 1)
                if x_ >= 2:
                    until(a_, l, "p_T", x_ - 1)
                w = TOK if t < NL else P
                a_.activation(Pm[:, x_ % 2, 0:w], PP(2 * (x_ % 2), P, w), ACT.Exp, bias=nb[:, x_:x_ + 1],
                              scale=sml[:, 16 + t:17 + t], accum_out=rsum[:, x_:x_ + 1]).then_inc(S["p_exp"].sem, 1)

            def pt(x_):
                t = x_ // H_MLA
                until(a_, l, "p_T", x_ + 1)
                if x_ >= 2:
                    until(a_, l, "pv", x_ - 1)
                w = 512 if t < NL else P
                a_.activation(PT[:, x_ % 2, 0:w], PS[:, 4, 0:w], ACT.Copy).then_inc(S["pt_a"].sem, 1)

            until(a_, l, "rs_q", 3)
            probs(0)
            for x_ in range(40):
                if x_ + 1 < 40:
                    probs(x_ + 1)
                pt(x_)
            for t in range(NT):
                if t >= 2:
                    until(a_, l, "g_mul", t - 1)
                else:
                    until(a_, l, "ret_tables", 160)
                a_.activation(gs[:, t % 2, :], gts[:, t, :], ACT.Silu).then_inc(S["g_silu"].sem, 1)
                gn_square(a_, l, t)
            rwkv_scalar(a_, l)

        def gn_square(a_, l, x_):
            until(a_, l, "gn_centred", x_ + 1)
            if x_ % 5 >= 2:
                until(a_, l, "gn_ss", x_ - 1)
            yc_, sqg_, _ = GN[x_ // NT]
            a_.activation(sqg_[:, x_ % 2, :], yc_[:, x_ % 2, :], ACT.Square).then_inc(S["gn_sq"].sem, 1)

        def second_half_out(v_, l, q):
            n, j = 3 * l + 1, q % 2
            v_.wait_ge(s_ea, u0(n) + q + 1)
            src = PP(3 * j + 1, 256, TOK)
            if q == 1:
                v_.tensor_copy(mz[0:64, 3, :], src[0:64, :]).then_inc(s_eb, 1)
            elif q < 1 or q in (6, 7):
                dst = {0: mz[:, 1, :], 6: rqk[:, 1, :], 7: rqk[:, 3, :]}[q]
                v_.tensor_copy(dst, src).then_inc(s_eb, 1)
            elif q < 8:
                f = {2: RW_R + 1, 3: RW_K + 1, 4: RW_V + 1, 5: RW_ZA}[q]
                v_.tensor_copy(rwz[:, f, 1:1 + LAT], src[:, 0:LAT])
                v_.tensor_copy(rwz[:, f, 2 + LAT:2 + TOK], src[:, LAT:TOK]).then_inc(s_eb, 1)
            elif q == 8:
                v_.tensor_copy(rwz[:, RW_ZG, 1 + 384:1 + LAT], PS[:, 3 * j + 1, 0:P])
                v_.tensor_copy(rwz[:, RW_ZG, 2 + LAT:2 + TOK], PS[:, 3 * j + 1, P:2 * P]).then_inc(s_eb, 1)
            else:
                dst = retv if q == 11 else gts[:, :, (q - 9) * 256:(q - 8) * 256]
                v_.tensor_copy(dst[:, 2:5, :], PP(3 * j + 1, 0, 768).rearrange("p (t n) -> p t n", t=3)).then_inc(s_eb, 1)

        def gn_stats(v_, l, x_, src):
            yc_, _, gst_ = GN[x_ // NT]
            sl = x_ % 2
            v_.reduce_sum(gst_[:, sl, 0, :].rearrange("p (q r) -> p q r", r=2), src, AX).then_inc(S["gn_sum"].sem, 1)
            until(v_, l, "gn_sum", x_ + 1)
            v_.tensor_scalar(gst_[:, sl, 1, :], gst_[:, sl, 0, :], -1.0 / HD, None, ALU.mult).then_inc(S["gn_mean"].sem, 1)
            until(v_, l, "gn_mean", x_ + 1)
            v_.tensor_tensor(yc_[:, sl, :].rearrange("p (q r v) -> p q r v", r=2, v=HD), src,
                             gst_[:, sl, 1, :].rearrange("p (q r) -> p q r", r=2).unsqueeze(3)
                             .broadcast_to([P, 4, 2, HD]), ALU.add)\
                .then_inc(S["gn_centred"].sem, 1)

        def gn_squares(v_, l, x_):
            _, sqg_, gst_ = GN[x_ // NT]
            until(v_, l, "gn_sq", x_ + 1)
            v_.reduce_sum(gst_[:, x_ % 2, 2, :], sqg_[:, x_ % 2, :].rearrange("p (g v) -> p g v", v=HD), AX)\
                .then_inc(S["gn_ss"].sem, 1)

        def gn_scale(v_, l, x_):
            yc_, _, gst_ = GN[x_ // NT]
            until(v_, l, "gn_rs", x_ + 1)
            y8 = yc_[:, x_ % 2, :].rearrange("p (g v) -> p g v", v=HD)
            v_.tensor_tensor(y8, y8, gst_[:, x_ % 2, 3, :].unsqueeze(2).broadcast_to([P, 8, HD]), ALU.mult)\
                .then_inc(S["gn_scaled"].sem, 1)

        def mix_vector(v_, l):
            n = 3 * l + 1
            mm_ = lambda name, k: until(v_, l, name, k)
            v_.wait_ge(s_eb, u0(n) + UNITS["mix"])
            mm_("ss_qkv", 1)
            v_.tensor_scalar(sml[:, 0:NT], PS[:, 7, 0:NT], 1.0 / QL, NORM_EPS, ALU.mult, ALU.add)\
                .then_inc(S["ms_q"].sem, 1)
            mm_("ss_qkv", 2)
            v_.tensor_scalar(rtmp[:], PP(4, P, TOK), 1.0 / KVL, NORM_EPS, ALU.mult, ALU.add).then_inc(S["ms_kv"].sem, 1)

            def q_rope(h):
                mm_("q_mm", h + 1)
                at = 2 * (h % 2) * 512 + P
                if h:
                    mm_("q_rope", 3 * h)
                v_.tensor_tensor(Pm[64:96, 1, :], PSF[96:128, at:at + TOK], sinm[96:128, :], ALU.mult)\
                    .then_inc(S["q_rope"].sem, 1)
                v_.tensor_tensor(QT[64:96, h, :], PSF[64:96, at:at + TOK], cosm[64:96, :], ALU.mult)\
                    .then_inc(S["q_rope"].sem, 1)

            def q_rope_add(h):
                mm_("q_rope", 3 * h + 2)
                v_.tensor_tensor(QT[64:96, h, :], QT[64:96, h, :], Pm[64:96, 1, :], ALU.add)\
                    .then_inc(S["q_rope"].sem, 1)

            mm_("mla_tables", 64)
            for h in range(2):
                q_rope(h)
                q_rope_add(h)
            mm_("rt_kv", 1)
            v_.reciprocal(rtmp[:], rtmp[:]).then_inc(S["rc_kv"].sem, 1)
            mm_("rc_kv", 1)
            v_.scalar_tensor_tensor(out=ckvT[:, PAST:PAST + TOK], in0=mz[:, 2, :], scalar=mcol[:, C_GKV:C_GKV + 1],
                                    in1=rtmp[:], op0=ALU.mult, op1=ALU.mult).then_inc(S["ckv"].sem, 1)
            v_.tensor_tensor(Pm[0:32, 0, :], mz[32:64, 3, :], sinm[32:64, :], ALU.mult).then_inc(S["kr"].sem, 1)
            v_.tensor_tensor(krT[0:32, PAST:], mz[0:32, 3, :], cosm[0:32, :], ALU.mult).then_inc(S["kr"].sem, 1)
            for h in range(2, H_MLA):
                q_rope(h)
                q_rope_add(h)
            mm_("kr", 2)
            v_.tensor_tensor(krT[0:32, PAST:], krT[0:32, PAST:], Pm[0:32, 0, :], ALU.add).then_inc(S["kr"].sem, 1)
            mm_("kr", 3)
            mm_("mla_weights", 48)
            v_.tensor_copy(KT[64:96, :, :], krT[0:32, :].unsqueeze(1).broadcast_to([32, H_MLA, PAST + TOK]))\
                .then_inc(S["kr_all"].sem, 1)
            mm_("co_T", 1)
            v_.tensor_copy(co[:], PS[:, 7, 0:KVL + ROPE]).then_inc(S["co"].sem, 1)
            for hp in range(4):
                mm_("k_mm", hp + 1)
                b = 2 * (hp % 2) * 512 + P
                v_.tensor_copy(KT[0:NOPE, 2 * hp + 1, :], PSF[NOPE:P, b:b + 768]).then_inc(S["k_odd"].sem, 1)

            def row_max(x_):
                t = x_ // H_MLA
                mm_("s_mm", x_ + 1)
                v_.reduce_max(mx[:, x_:x_ + 1], PP(2 * (x_ % 2), P, TOK if t < NL else P), AX).then_inc(S["s_max"].sem, 1)
                mm_("s_max", x_ + 1)
                v_.tensor_scalar(nb[:, x_:x_ + 1], mx[:, x_:x_ + 1], sml[:, 16 + t:17 + t], -1.0, ALU.mult, ALU.mult)\
                    .then_inc(S["s_bias"].sem, 1)

            def pt(x_):
                if x_ >= 32:
                    return
                mm_("p_T", x_ + 1)
                if x_ >= 2:
                    mm_("pv", x_ - 1)
                v_.tensor_copy(PT[:, x_ % 2, 512:TOK], PS[:, 5, 0:P]).then_inc(S["pt_b"].sem, 1)

            def out(t):
                mm_("pv", 8 * (t + 1))
                v_.reciprocal(rinv[:, 8 * t:8 * t + 8], rsum[:, 8 * t:8 * t + 8]).then_inc(S["r_inv"].sem, 1)
                mm_("r_inv", t + 1)
                v_.tensor_tensor(mla_o[:, t, :].rearrange("p (h v) -> p h v", v=VHD),
                                 PS[:, 6 + t % 2, :].rearrange("p (h v) -> p h v", v=VHD),
                                 rinv[:, 8 * t:8 * t + 8].unsqueeze(2).broadcast_to([P, H_MLA, VHD]), ALU.mult)\
                    .then_inc(S["o_out"].sem, 1)

            mm_("rs_q", 3)
            row_max(0)
            row_max(1)
            for x_ in range(40):
                pt(x_)
                if x_ + 2 < 40:
                    row_max(x_ + 2)
                if x_ % 8 == 2 and x_ > 8:
                    out(x_ // 8 - 1)
            out(4)

            mm_("ret_tables", 160)
            for f in range(4):
                mm_("rot_mm", f + 1)
                if f >= 2:
                    mm_("roped", f - 1)
                v_.tensor_tensor(rot[:, f % 2, :], PP(2 * (f % 2), P, TOK), sinr[:], ALU.mult).then_inc(S["rot_sin"].sem, 1)
                if f:
                    mm_("rot_cos", f)
                    mm_("rot_sin", f)
                    v_.tensor_tensor(rqk[:, f - 1, :], rqk[:, f - 1, :], rot[:, (f - 1) % 2, :], ALU.add)\
                        .then_inc(S["roped"].sem, 1)
            mm_("rot_cos", 4)
            mm_("rot_sin", 4)
            v_.tensor_tensor(rqk[:, 3, :], rqk[:, 3, :], rot[:, 1, :], ALU.add).then_inc(S["roped"].sem, 1)
            for t in range(NT + 1):
                if t < NT:
                    mm_("kt_T", t + 1)
                    v_.tensor_copy(ktok[:, t, :], PS[:, 4 + t % 2, 0:DR]).then_inc(S["kt_out"].sem, 1)
                if t:
                    mm_("kv_mm", t)
                    v_.tensor_copy(kvs[:, t - 1, :, :, :].rearrange("p d f v -> p (d f v)"),
                                   PS[:, 6 + (t - 1) % 2, 0:256]).then_inc(S["kv_out"].sem, 1)
            mm_("kv_out", 5)
            for c in range(NL - 1):
                if c:
                    mm_("ret_chain", 4 * c)
                for d, a, b in ((0, c, c + 1), (1, NL - 1 - c, NL - 2 - c)):
                    for ft in range(2):
                        v_.scalar_tensor_tensor(out=Rall[:, b, d, ft, :], in0=Rall[:, a, d, ft, :],
                                                scalar=gch[:, d, ft:ft + 1], in1=kvs[:, a, d, ft, :], op0=ALU.mult,
                                                op1=ALU.add).then_inc(S["ret_chain"].sem, 1)

            def masked(t):
                mm_("rs_mm", t + 1)
                if t >= 2:
                    mm_("ro_mm", t - 1)
                for pr in range(2):
                    m = v_.tensor_tensor(Sm[:, t % 2, pr:NH:2, :, :],
                                         PS[:, t % 2 + 4 * pr, 0:256].rearrange("p (f n) -> p f n", f=2).unsqueeze(2)
                                         .broadcast_to([P, 2, 2, P]), dmask[:, pr:NH:2, :, :], ALU.mult)
                m.then_inc(S["rs_masked"].sem, 1)

            def finish(t):
                mm_("gn_ss", t + 1)
                gn_scale(v_, l, t)
                mm_("gn_scaled", t + 1)
                mm_("g_gain", t + 1)
                v_.tensor_tensor(yc[:, t % 2, :], yc[:, t % 2, :], gs[:, t % 2, :], ALU.mult).then_inc(S["g_mul"].sem, 1)
                mm_("g_mul", t + 1)
                v_.tensor_tensor(retv[:, t, :], yc[:, t % 2, 0:DR], yc[:, t % 2, DR:], ALU.add)\
                    .then_inc(S["ret_o"].sem, 1)

            masked(0)
            for t in range(NT):
                if t + 1 < NT:
                    masked(t + 1)
                mm_("ro_mm", t + 1)
                if t >= 2:
                    mm_("ret_o", t - 1)
                gn_stats(v_, l, t, PS[:, 2 + 4 * (t % 2):4 + 4 * (t % 2), 0:256].rearrange("p r (q v) -> p q r v", v=HD))
                gn_squares(v_, l, t)
                if t:
                    finish(t - 1)
            finish(NT - 1)
            rwkv_vector(v_, l)

        def gn_pool(po, l, x_, eps):
            gst_ = GN[x_ // NT][2]
            until(po, l, "gn_ss", x_ + 1)
            po.tensor_scalar(gst_[:, x_ % 2, 2, :], gst_[:, x_ % 2, 2, :], 1.0 / HD, eps, ALU.mult, ALU.add)\
                .then_inc(S["gn_ms"].sem, 1)
            until(po, l, "gn_ms", x_ + 1)
            po.tensor_tensor(gst_[:, x_ % 2, 3, :], gst_[:, x_ % 2, 2, :], powe[:], ALU.pow).then_inc(S["gn_rs"].sem, 1)

        def mix_gpsimd(po, l):
            until(po, l, "ms_q", 1)
            po.tensor_tensor(sml[:, 8:8 + NT], sml[:, 0:NT], powe[:, 0:NT], ALU.pow).then_inc(S["rs_q"].sem, 1)
            until(po, l, "rs_q", 1)
            po.tensor_scalar(sml[:, 16:16 + NT], sml[:, 8:8 + NT], MLA_SCALE, None, ALU.mult).then_inc(S["rs_q"].sem, 2)
            until(po, l, "ret_tables", 160)
            for f in range(4):
                until(po, l, "rot_mm", f + 1)
                po.tensor_tensor(rqk[:, f, :], rqk[:, f, :], cosr[:], ALU.mult).then_inc(S["rot_cos"].sem, 1)
            for t in range(NT):
                if t >= 2:
                    until(po, l, "kv_mm", t - 1)
                po.tensor_tensor(vz[:, t % 2, :, :, :],
                                 retv[:, t, :].rearrange("p (h v) -> p h v", v=HD).unsqueeze(2)
                                 .broadcast_to([P, NH, 2, HD]),
                                 zeta[:].unsqueeze(3).broadcast_to([P, NH, 2, HD]), ALU.mult)\
                    .then_inc(S["v_decayed"].sem, 1)
            until(po, l, "roped", 4)
            for t in range(NT):
                if t < NL:
                    if t >= 2:
                        until(po, l, "ro_mm", t - 1)
                    po.tensor_tensor(qxi[:, t % 2, :, :, :],
                                     rqk[:, 0:2, t * P:(t + 1) * P].unsqueeze(1).broadcast_to([P, 2, 2, P]),
                                     xi[:], ALU.mult).then_inc(S["q_decayed"].sem, 1)
                until(po, l, "g_silu", t + 1)
                po.tensor_tensor(gs[:, t % 2, :], gs[:, t % 2, :], rgn[:], ALU.mult).then_inc(S["g_gain"].sem, 1)
                gn_pool(po, l, t, RET_EPS)
            rwkv_gpsimd(po, l)

        def rows(h):
            return slice((h % 2) * HD, (h % 2 + 1) * HD)

        def shift_scalar(a_, l, f):
            until(a_, l, "mu_cols", 4)
            until(a_, l, "pads", 1)
            until(a_, l, "nbr_sum", f + 1)
            a_.activation(rwz[:, f, 1:RWW - 1], rwz[:, f, 1:RWW - 1], ACT.Copy, scale=mcon[:, 0, f:f + 1])\
                .then_inc(S["own_part"].sem, 1)

        def shift_vector(v_, l, f):
            until(v_, l, "pads", 1)
            until(v_, l, "mu_cols", 4)
            v_.wait_ge(s_ea, u0(3 * l + 1) + (9 if f == RW_ZG else 6))
            v_.wait_ge(s_eb, u0(3 * l + 1) + (9 if f == RW_ZG else 6))
            if f >= 2:
                until(v_, l, "shifted", f - 1)
            v_.tensor_tensor(ssh[:, f % 2, 1:RWW - 1], rwz[:, f, 0:RWW - 2], rwz[:, f, 2:RWW], ALU.add)\
                .then_inc(S["nbr_sum"].sem, 1)
            until(v_, l, "own_part", f + 1)
            until(v_, l, "nbr_sum", f + 1)
            v_.scalar_tensor_tensor(out=rwz[:, f, 1:RWW - 1], in0=ssh[:, f % 2, 1:RWW - 1], scalar=mcon[:, 1, f:f + 1],
                                    in1=rwz[:, f, 1:RWW - 1], op0=ALU.mult, op1=ALU.add).then_inc(S["shifted"].sem, 1)

        def shift_gpsimd(po, l):
            until(po, l, "mix_columns", 16)
            po.tensor_scalar(mcon[:, 0, :], mcol[:, C_MU:C_MU + NRW], -1.0, 1.0, ALU.mult, ALU.add)\
                .then_inc(S["mu_cols"].sem, 1)
            po.tensor_scalar(mcon[:, 1, :], mcol[:, C_MU:C_MU + NRW], 0.5, None, ALU.mult).then_inc(S["mu_cols"].sem, 1)
            po.tensor_scalar(half[:, 0:4], mcol[:, C_AB:C_AB + 4], 0.5, None, ALU.mult).then_inc(S["mu_cols"].sem, 1)
            po.tensor_scalar(sml[:, 32:34], mcol[:, C_V5:C_V5 + 2], -1.0, 1.0, ALU.mult, ALU.add)\
                .then_inc(S["mu_cols"].sem, 1)
            low_part_done(po, 3 * l + 1, NT - 1)
            low_part_done(po, 3 * l + 1, NT - 2)
            po.memset(rwz[:, :, 0:1], 0.0)
            po.memset(rwz[:, :, 1 + LAT:2 + LAT], 0.0)
            po.memset(rwz[:, :, RWW - 2:RWW], 0.0).then_inc(S["pads"].sem, 1)

        def rwkv_tensor(pe, l):
            until(pe, l, "kk_sq", 1)
            until(pe, l, "rwkv_tables", 16 * 11)
            for ft in range(2):
                for a, z in ((0, 512), (512, RWW)):
                    mm = pe.matmul(PS[:, 2 * ft + a // 512, 0:z - a], blk[:], ksq[:, ft, a:z], start=True, stop=True)
            mm.then_inc(S["kk_ss"].sem, 1)

            def prep(c, part):
                cols = slice(rw_col(c), rw_col(c) + P)
                if part == 0:
                    if c:
                        until(pe, l, "alpha_tok", c)
                        until(pe, l, "beta_tok", c)
                    else:
                        until(pe, l, "lora_act", 2)
                        until(pe, l, "kk_rt", 1)
                        until(pe, l, "shifted", 9)
                    for d in range(2):
                        r = rows(d)
                        pe.matmul(PS[:, d, 0:DR], rwz[r, RW_ZW, cols], upw[r, :], start=True, stop=True)
                        for ft in range(2):
                            mm = pe.matmul(PS[:, d, DR + ft * P:DR + (ft + 1) * P], upa[r, ft * P:(ft + 1) * P],
                                           rwz[r, RW_ZA, cols], start=True, stop=True)
                    mm.then_inc(S["wa_mm"].sem, 1)
                elif part == 1:
                    until(pe, l, "w_sig", c + 1)
                    if c:
                        until(pe, l, "kappa_tok", c)
                        until(pe, l, "v_tok", c)
                        until(pe, l, "bv", c)
                    for d in range(2):
                        for ft in range(2):
                            mm = pe.matmul(PS[:, 2 + d, ft * 256:(ft + 1) * 256],
                                           sgw[:, d * DR + ft * P:d * DR + (ft + 1) * P], tri[:, d, :], start=True,
                                           stop=True)
                    mm.then_inc(S["cs_mm"].sem, 1)
                else:
                    s = c % 2
                    until(pe, l, "alpha", c + 1)
                    until(pe, l, "beta", c + 1)
                    until(pe, l, "kappa", c + 1)
                    until(pe, l, "rk", c + 1)
                    until(pe, l, "decays", c + 1)
                    until(pe, l, "p_inv", c + 1)
                    for d in range(2):
                        for ft in range(2):
                            q = 2 * d + ft
                            at = slice(q * P, (q + 1) * P)
                            pe.transpose(PS[:, 0, at], E[s][:, d, ft, 0, :], ident[:])
                            pe.transpose(PS[:, 1, at], ab[:, d, ft, :], ident[:])
                            pe.transpose(PS[:, 2, at], kd[:, d, ft, :], ident[:])
                    for ft in range(2):
                        pe.transpose(PS[:, 3, ft * P:(ft + 1) * P], rwz[:, RW_V + ft, cols], ident[:])
                        mm = pe.matmul(PS[:, 3, 256 + 2 * ft:258 + 2 * ft], rk[:, ft, :], hsel[:], start=True, stop=True)
                    mm.then_inc(S["tok_T"].sem, 1)

            def inner(c, which):
                s = c % 2
                src, name = ((ab, "lb"), (kd, "lk"))[which]
                for d in range(2):
                    if which:
                        until(pe, l, f"lb{d}", c + 1)
                    elif c:
                        until(pe, l, f"yl_out{d}", c)
                        until(pe, l, f"n_out{d}", c)
                    else:
                        until(pe, l, "alpha", c + 1)
                        if l == 0 and d == 0:
                            until(pe, l, "ret_o", 5)
                    until(pe, l, "rho", c + 1)
                    for h in range(NH):
                        r = rows(h)
                        mm = pe.matmul(PS[:, 4 + 2 * d + h % 2, (h // 2) * 256:(h // 2 + 1) * 256],
                                       src[r, d, h // 2, :], E[s][r, d, h // 2, :, :], start=True, stop=True)
                    mm.then_inc(S[f"{name}_mm{d}"].sem, 1)

            def group(bank, width, lhs, rhs):
                for h in range(NH):
                    mm = pe.matmul(PS[:, bank, h * width:(h + 1) * width], lhs(h), rhs(h), start=True, stop=True)
                return mm

            def solve(c):
                s = c % 2
                inner(c, 0)
                inner(c, 1)
                for d in range(2):
                    until(pe, l, f"lm{d}", 7 * c + 1)
                    until(pe, l, f"lk{d}", c + 1)
                    for h in range(NH):
                        mm = pe.transpose(PS[:, 4 + 2 * d, h * P:(h + 1) * P], LM[d][:, h, :], ident[:])
                    mm.then_inc(S[f"lm_T{d}"].sem, 1)
                for d in range(2):
                    until(pe, l, "v_tok", c + 1)
                    group(5 + 2 * d, HD, lambda h: LK[d][:, h, 0, :], lambda h: vtok[:, s, h * HD:(h + 1) * HD])\
                        .then_inc(S[f"lv_mm{d}"].sem, 1)
                for lv in range(1, 7):
                    for d in range(2):
                        until(pe, l, f"lm{d}", 7 * c + lv + 1)
                        until(pe, l, f"x{d}", 6 * c + lv)
                        until(pe, l, f"xt{d}", 7 * c + lv)
                        group(4 + 2 * d, P, lambda h: LM[d][:, h, :], lambda h: X[d][:, h, :])\
                            .then_inc(S[f"t1_mm{d}"].sem, 1)
                    for d in range(2):
                        until(pe, l, f"t1{d}", 6 * c + lv)
                        if lv < 6:
                            if lv == 1:
                                until(pe, l, f"lv{d}", c + 1)
                            group(5 + 2 * d, P, lambda h: XT[d][:, h, :], lambda h: T1[d][:, h, :])\
                                .then_inc(S[f"dx_mm{d}"].sem, 1)
                        group(4 + 2 * d, P, lambda h: T1[d][:, h, :], lambda h: XT[d][:, h, :])\
                            .then_inc(S[f"dxt_mm{d}"].sem, 1)
                    if c + 1 < NT and lv in (1, 3, 5):
                        prep(c + 1, (1, 3, 5).index(lv))
                for d in range(2):
                    until(pe, l, f"xt{d}", 7 * c + 7)
                    until(pe, l, "alpha_tok", c + 1)
                    until(pe, l, f"lv{d}", c + 1)
                    group(5 + 2 * d, P, lambda h: XT[d][:, h, :], lambda h: R[s][d][:, h, :])\
                        .then_inc(S[f"gh_mm{d}"].sem, 1)
                for d in range(2):
                    until(pe, l, f"gh{d}", c + 1)
                    until(pe, l, "beta_tok", c + 1)
                    until(pe, l, "kappa_tok", c + 1)
                    for h in range(NH):
                        ft, r = h // 2, rows(h)
                        G, H = X[d][:, h, 0:HD], X[d][:, h, HD:P]
                        b, v = btok[:, s, d, h * HD:(h + 1) * HD], vtok[:, s, h * HD:(h + 1) * HD]
                        bank = PS[r, 4 + 2 * d, :]
                        if c < NL:
                            pe.matmul(bank[:, ft * P:(ft + 1) * P], G, LB[d][:, h, 1, :], start=True, stop=True)
                            pe.matmul(bank[:, 256 + ft * HD:256 + (ft + 1) * HD], G, b, start=True, stop=True)
                        at = 384 + ft * HD
                        pe.matmul(bank[:, at:at + HD], b, H, start=True, stop=False)
                        mm = pe.matmul(bank[:, at:at + HD], kptok[:, s, d, h * HD:(h + 1) * HD], v, start=False, stop=True)
                    mm.then_inc(S[f"fin_mm{d}"].sem, 1)
                    for h in range(NH):
                        dst = PS[:, 5 + 2 * d, h * HD:(h + 1) * HD]
                        pe.matmul(dst, LB[d][:, h, 1, :], X[d][:, h, HD:P], start=True, stop=False)
                        mm = pe.matmul(dst, LK[d][:, h, 1, :], vtok[:, s, h * HD:(h + 1) * HD], start=False, stop=True)
                    mm.then_inc(S[f"yl_mm{d}"].sem, 1)

            for part in range(3):
                prep(0, part)
            for c in range(NT):
                solve(c)
            until(pe, l, "rwkv_states", 32)
            for d in range(2):
                until(pe, l, f"n_out{d}", 5)
                until(pe, l, f"rg_out{d}", 4)
                until(pe, l, f"mt_out{d}", 4)
                until(pe, l, f"yl_out{d}", 5)
            until(pe, l, "bv", 5)
            until(pe, l, "v_tok", 5)
            until(pe, l, "alpha_tok", 5)
            for c in range(NL - 1):
                if c:
                    until(pe, l, "st_out", c)
                for d, t in ((0, c), (1, NL - 1 - c)):
                    for h in range(NH):
                        ft, r = h // 2, rows(h)
                        at = (2 * d + ft) * HD
                        mm = pe.matmul(PS[r, c % 2, at:at + HD], MTs[r, t, d, ft, :], STa[r, t, d, ft, :], start=True,
                                       stop=True)
                mm.then_inc(S["st_mm"].sem, 1)
            for t in range(NT):
                if t < NL:
                    until(pe, l, "st_out", 3)
                    if t >= 2:
                        until(pe, l, "y_sum", t - 1)
                    for d in range(2):
                        for h in range(NH):
                            ft, r = h // 2, rows(h)
                            at = (2 * d + ft) * HD
                            mm = pe.matmul(PS[:, 4 + 2 * (t % 2) + h % 2, at:at + HD], RGs[r, t, d, ft, :], STa[r, t, d, ft, :],
                                           start=True, stop=True)
                    mm.then_inc(S["y_mm"].sem, 1)
                if t >= 2:
                    until(pe, l, "rwkv_o", t - 1)
                pe.matmul(PS[:, t % 2, 0:DR], rwz[:, RW_ZG, rw_col(t):rw_col(t) + P], gup[:], start=True, stop=True)\
                    .then_inc(S["gate_mm"].sem, 1)
            for t in range(NT):
                until(pe, l, "rwkv_o", t + 1)
                if t >= 2:
                    until(pe, l, "mixT_a", t - 1)
                    until(pe, l, "mixT_b", t - 1)
                b = 4 + 2 * (t % 2)
                for k in range(KD):
                    src = mla_o[:, t, k * P:(k + 1) * P] if k < 4 else Yls[:, t, (k - 4) * P:(k - 3) * P] if k < 6 \
                        else retv[:, t, (k - 6) * P:(k - 5) * P]
                    mm = pe.transpose(PS[:, b + k // 4, (k % 4) * P:(k % 4 + 1) * P], src, ident[:])
                mm.then_inc(S["mixT_mm"].sem, 1)

        def rwkv_scalar(a_, l):
            until(a_, l, "shifted", 9)
            until(a_, l, "ret_o", 5)
            for ft in range(2):
                a_.activation(kk[:, ft, :], rwz[:, RW_K + ft, :], ACT.Copy, scale=mcol[:, C_V4 + ft:C_V4 + ft + 1])\
                    .then_inc(S["kk_gain"].sem, 1)
            until(a_, l, "kk_gain", 2)
            a_.activation(ksq[:], kk[:], ACT.Square).then_inc(S["kk_sq"].sem, 1)
            for f in (RW_ZW, RW_ZG):
                a_.activation(rwz[:, f, :], rwz[:, f, :], ACT.Tanh, scale=1.0 if f == RW_ZW else 0.5)\
                    .then_inc(S["lora_act"].sem, 1)
            until(a_, l, "kk_ss", 1)
            a_.activation(knorm[:, :, 0:512], PSF[:, 0:2048].rearrange("p (f n) -> p f n", f=2)[:, :, 0:512], ACT.Sqrt)
            a_.activation(knorm[:, :, 512:RWW],
                          PSF[:, 0:2048].rearrange("p (f n) -> p f n", f=2)[:, :, 512:RWW], ACT.Sqrt)\
                .then_inc(S["kk_rt"].sem, 1)

            def prep(c, part):
                s = c % 2
                if part == 0:
                    until(a_, l, "w_bias", c + 1)
                    a_.activation(sgw[:], sgw[:], ACT.Tanh, scale=0.5).then_inc(S["w_tanh"].sem, 1)
                    if c:
                        for d in range(2):
                            until(a_, l, f"lb_mm{d}", c)
                        until(a_, l, "tok_T", c)
                    else:
                        until(a_, l, "kk", 1)
                    for d in range(2):
                        for ft in range(2):
                            q = 2 * d + ft
                            m = a_.activation(ab[:, d, ft, :], PS[:, d, DR + ft * P:DR + (ft + 1) * P], ACT.Tanh,
                                              bias=half[:, q:q + 1], scale=0.5)
                    m.then_inc(S["a_tanh"].sem, 1)
                elif part == 1:
                    until(a_, l, "cs_mm", c + 1)
                    if c >= 2:
                        for d in range(2):
                            until(a_, l, f"rg_out{d}", c - 1)
                            until(a_, l, f"fin_mm{d}", c - 1)
                    m = a_.activation(E[s][:].rearrange("p d f e t -> p (d f e t)"), PSF[:, 1024:2048], ACT.Exp)
                    m.then_inc(S["decays"].sem, 1)
                    if c:
                        until(a_, l, "kappa", c)
                        until(a_, l, "beta", c)
                    a_.activation(Pinv[:].rearrange("p d f t -> p (d f) t"),
                                  PSF[:, 1024:2048].rearrange("p (q e t) -> p q e t", q=4, e=2)[:, :, 1, :],
                                  ACT.Exp, scale=-1.0).then_inc(S["p_inv"].sem, 1)
                else:
                    until(a_, l, "tok_T", c + 1)
                    if c >= 2:
                        for d in range(2):
                            until(a_, l, f"gh_mm{d}", c - 1)
                            until(a_, l, f"fin_mm{d}", c - 1)
                    for d in range(2):
                        m = a_.activation(R[s][d][:, :, 0:HD],
                                          PS[:, 0, d * DR:(d + 1) * DR].rearrange("p (h k) -> p h k", h=NH), ACT.Copy)
                    m.then_inc(S["alpha_tok"].sem, 1)
                    a_.activation(kptok[:, s, :, :], PS[:, 2, :].rearrange("p (d n) -> p d n", d=2), ACT.Copy)\
                        .then_inc(S["kappa_tok"].sem, 1)

            def solve(c):
                s = c % 2
                for d in range(2):
                    until(a_, l, f"lv_mm{d}", c + 1)
                    a_.activation(R[s][d][:, :, HD:P], PS[:, 5 + 2 * d, 0:DR].rearrange("p (h v) -> p h v", h=NH),
                                  ACT.Copy).then_inc(S[f"lv{d}"].sem, 1)
                for lv in range(1, 7):
                    for d in range(2):
                        until(a_, l, f"t1_mm{d}", 6 * c + lv)
                        if lv > 1:
                            until(a_, l, f"dxt_mm{d}", 6 * c + lv - 1)
                        a_.activation(T1[d][:].rearrange("p h t -> p (h t)"), PS[:, 4 + 2 * d, :], ACT.Copy)\
                            .then_inc(S[f"t1{d}"].sem, 1)
                    if c + 1 < NT and lv in (2, 4, 6):
                        prep(c + 1, (2, 4, 6).index(lv))
                for d in range(2):
                    until(a_, l, f"gh_mm{d}", c + 1)
                    a_.activation(X[d][:].rearrange("p h t -> p (h t)"), PS[:, 5 + 2 * d, :], ACT.Copy)\
                        .then_inc(S[f"gh{d}"].sem, 1)
                for d in range(2):
                    until(a_, l, f"yl_mm{d}", c + 1)
                    a_.activation(Yls[:, c, d * DR:(d + 1) * DR], PS[:, 5 + 2 * d, 0:DR], ACT.Copy)\
                        .then_inc(S[f"yl_out{d}"].sem, 1)

            for part in range(3):
                prep(0, part)
            for c in range(NT):
                solve(c)
            for t in range(NT):
                gn_square(a_, l, NT + t)
            for t in range(NT):
                until(a_, l, "mixT_mm", t + 1)
                a_.activation(act[:, 0:4, t * P:(t + 1) * P], PS[:, 4 + 2 * (t % 2), :].rearrange("p (k t) -> p k t", k=4),
                              ACT.Copy).then_inc(S["mixT_a"].sem, 1)
            until(a_, l, "mixT_a", 5)
            until(a_, l, "mixT_b", 5)
            until(a_, l, "mix_stored", 64)

        def rwkv_vector(v_, l):
            mm_ = lambda name, k: until(v_, l, name, k)
            mm_("lora_act", 2)
            v_.tensor_scalar(rwz[:, RW_ZG, :], rwz[:, RW_ZG, :], 0.5, 0.5, ALU.mult, ALU.add).then_inc(S["zg_sig"].sem, 1)
            mm_("kk_rt", 1)
            v_.tensor_scalar(knorm[:], knorm[:], 1e-12, None, ALU.add).then_inc(S["kk_inv"].sem, 1)
            mm_("kk_inv", 1)
            v_.reciprocal(knorm[:], knorm[:]).then_inc(S["kk_inv"].sem, 1)
            mm_("kk_inv", 2)
            v_.tensor_tensor(kk[:], kk[:], knorm[:], ALU.mult).then_inc(S["kk"].sem, 1)
            mm_("kk", 1)
            mm_("mix_stored", 48)
            mm_("rwkv_tables", 16 * 11)

            def prep(c, part):
                s = c % 2
                cols = slice(rw_col(c), rw_col(c) + P)
                bc = lambda t: t.unsqueeze(1).broadcast_to([P, 2, 2, P])
                if part == 0:
                    mm_("wa_mm", c + 1)
                    if c:
                        mm_("cs_mm", c)
                    v_.tensor_tensor(sgw[:].rearrange("p (d n) -> p d n", d=2), PS[:, 0:2, 0:DR],
                                     v01[:].rearrange("p (d n) -> p d n", d=2), ALU.add).then_inc(S["w_bias"].sem, 1)
                elif part == 1:
                    mm_("w_tanh", c + 1)
                    v_.tensor_scalar(sgw[:], sgw[:], 0.5, 0.5, ALU.mult, ALU.add).then_inc(S["w_sig"].sem, 1)
                    mm_("a_tanh", c + 1)
                    v_.tensor_scalar(ab[:], ab[:], 0.5, 0.5, ALU.mult, ALU.add).then_inc(S["a_sig"].sem, 1)
                elif part == 2:
                    mm_("decays", c + 1)
                    v_.tensor_copy(PCs[:, c, 0, :], E[s][:, 0, :, 1, P - 1])
                    v_.tensor_copy(PCs[:, c, 1, :], E[s][:, 1, :, 1, 0]).then_inc(S["pc"].sem, 1)
                    mm_("pc", c + 1)
                    v_.tensor_tensor(E[s][:, :, :, 0, :], E[s][:, :, :, 0, :], bc(kk[:, :, cols]), ALU.mult)\
                        .then_inc(S["alpha"].sem, 1)
                    v_.tensor_tensor(E[s][:, :, :, 1, :], E[s][:, :, :, 1, :], bc(rwz[:, RW_R:RW_R + 2, cols]), ALU.mult)\
                        .then_inc(S["rho"].sem, 1)
                    mm_("a_sig", c + 1)
                    mm_("kd_a", c + 1)
                    v_.tensor_tensor(ab[:], ab[:], bc(kk[:, :, cols]), ALU.mult).then_inc(S["b_a"].sem, 1)
                    mm_("p_inv", c + 1)
                    mm_("b_a", c + 1)
                    v_.scalar_tensor_tensor(out=ab[:], in0=ab[:], scalar=-1.0, in1=Pinv[:], op0=ALU.mult, op1=ALU.mult)\
                        .then_inc(S["beta"].sem, 1)
                    mm_("kd_sum", c + 1)
                    for ft in range(2):
                        m = v_.scalar_tensor_tensor(out=rk[:, ft, :], in0=rk[:, ft, :],
                                                    scalar=mcol[:, C_V6 + ft:C_V6 + ft + 1],
                                                    in1=rwz[:, RW_R + ft, cols], op0=ALU.mult, op1=ALU.mult)
                    m.then_inc(S["rk"].sem, 1)
                else:
                    mm_("tok_T", c + 1)
                    if c >= 2:
                        for d in range(2):
                            mm_(f"fin_mm{d}", c - 1)
                            mm_(f"yl_mm{d}", c - 1)
                        mm_("bv", c - 1)
                    v_.tensor_copy(btok[:, s, :, :].rearrange("p d n -> p (d n)"), PS[:, 1, :])\
                        .then_inc(S["beta_tok"].sem, 1)
                    v_.tensor_copy(vtok[:, s, :], PS[:, 3, 0:DR]).then_inc(S["v_tok"].sem, 1)
                    mm_("v_tok", c + 1)
                    v_.tensor_tensor(bv[:, c, :].rearrange("p (h v) -> p h v", h=NH),
                                     vtok[:, s, :].rearrange("p (h v) -> p h v", h=NH),
                                     PS[:, 3, 256:260].unsqueeze(2).broadcast_to([P, NH, HD]), ALU.mult)\
                        .then_inc(S["bv"].sem, 1)

            def solve(c):
                s = c % 2
                idb = ident[:].unsqueeze(1).broadcast_to([P, NH, P])
                for name, dst in (("lb", LB), ("lk", LK)):
                    for d in range(2):
                        mm_(f"{name}_mm{d}", c + 1)
                        if c:
                            mm_(f"yl_mm{d}", c)
                        for pr in range(2):
                            m = v_.tensor_tensor(dst[d][:, pr:NH:2, :, :],
                                                 PS[:, 4 + 2 * d + pr, :].rearrange("p (f e t) -> p f e t", f=2, e=2),
                                                 mask2[:, d, :, :].unsqueeze(1).broadcast_to([P, 2, 2, P]), ALU.mult)
                        m.then_inc(S[f"{name}{d}"].sem, 1)
                for d in range(2):
                    mm_(f"lm{d}", 7 * c + 1)
                    v_.tensor_tensor(XT[d][:], LM[d][:], idb, ALU.add).then_inc(S[f"xt{d}"].sem, 1)
                    mm_(f"lm_T{d}", c + 1)
                    v_.tensor_tensor(X[d][:], PS[:, 4 + 2 * d, :].rearrange("p (h t) -> p h t", h=NH), idb, ALU.add)\
                        .then_inc(S[f"x{d}"].sem, 1)
                for lv in range(1, 7):
                    for d in range(2):
                        if lv < 6:
                            mm_(f"dx_mm{d}", 5 * c + lv)
                            mm_(f"x{d}", 6 * c + lv)
                            v_.tensor_tensor(X[d][:].rearrange("p h t -> p (h t)"), X[d][:].rearrange("p h t -> p (h t)"),
                                             PS[:, 5 + 2 * d, :], ALU.add).then_inc(S[f"x{d}"].sem, 1)
                        mm_(f"dxt_mm{d}", 6 * c + lv)
                        mm_(f"xt{d}", 7 * c + lv)
                        v_.tensor_tensor(XT[d][:].rearrange("p h t -> p (h t)"), XT[d][:].rearrange("p h t -> p (h t)"),
                                         PS[:, 4 + 2 * d, :], ALU.add).then_inc(S[f"xt{d}"].sem, 1)
                    if c + 1 < NT and lv in (1, 2, 4, 6):
                        prep(c + 1, (1, 2, 4, 6).index(lv))
                for d in range(2):
                    mm_(f"fin_mm{d}", c + 1)
                    bank = PS[:, 4 + 2 * d, :]
                    if c < NL:
                        v_.tensor_tensor(MTs[:, c, d, :, :], bank[:, 256:384].rearrange("p (f k) -> p f k", f=2),
                                         id64[:].unsqueeze(1).broadcast_to([P, 2, HD]), ALU.add)\
                            .then_inc(S[f"mt_out{d}"].sem, 1)
                        v_.tensor_tensor(RGs[:, c, d, :, :], bank[:, 0:256].rearrange("p (f t) -> p f t", f=2),
                                         E[s][:, d, :, 1, :], ALU.add).then_inc(S[f"rg_out{d}"].sem, 1)
                    mm_("pc", c + 1)
                    for ft in range(2):
                        m = v_.tensor_scalar(Ns[:, c, d, ft, :], bank[:, 384 + ft * HD:384 + (ft + 1) * HD],
                                             PCs[:, c, d, ft:ft + 1], None, ALU.mult)
                    m.then_inc(S[f"n_out{d}"].sem, 1)

            for part in range(4):
                prep(0, part)
            for c in range(NT):
                solve(c)
            for d in range(2):
                mm_(f"n_out{d}", 5)
            for c in range(NL - 1):
                mm_("st_mm", c + 1)
                for d, a, b in ((0, c, c + 1), (1, NL - 1 - c, NL - 2 - c)):
                    for ft in range(2):
                        at = (2 * d + ft) * HD
                        m = v_.scalar_tensor_tensor(out=STa[:, b, d, ft, :], in0=PS[:, c % 2, at:at + HD],
                                                    scalar=PCs[:, a, d, ft:ft + 1], in1=Ns[:, a, d, ft, :], op0=ALU.mult,
                                                    op1=ALU.add)
                m.then_inc(S["st_out"].sem, 1)

            def finish(t):
                gn_scale(v_, l, NT + t)
                mm_("gn_scaled", NT + t + 1)
                o1 = rsumd[:, t % 2, :]
                if t >= 2:
                    mm_("rwkv_o", t - 1)
                v_.tensor_tensor(o1, yc2[:, (NT + t) % 2, 0:DR], yc2[:, (NT + t) % 2, DR:], ALU.add).then_inc(S["y_dirs"].sem, 1)
                mm_("y_dirs", t + 1)
                v_.tensor_tensor(o1, o1, v7[:], ALU.mult).then_inc(S["y_gain"].sem, 1)
                mm_("y_gain", t + 1)
                v_.tensor_tensor(o1, o1, bv[:, t, :], ALU.add).then_inc(S["y_bonus"].sem, 1)
                mm_("y_bonus", t + 1)
                mm_("gate_mm", t + 1)
                v_.tensor_tensor(Yls[:, t, 0:DR], PS[:, t % 2, 0:DR], o1, ALU.mult).then_inc(S["rwkv_o"].sem, 1)

            for d in range(2):
                mm_(f"yl_out{d}", 5)
                mm_(f"yl_mm{d}", 5)
            for t in range(NT):
                if t < NL:
                    mm_("y_mm", t + 1)
                    for pr in range(2):
                        own = Yls[:, t, :].rearrange("p (q r v) -> p q r v", r=2, v=HD)[:, :, pr, :]
                        m = v_.tensor_tensor(own, own, PS[:, 4 + 2 * (t % 2) + pr, 0:256]
                                             .rearrange("p (q v) -> p q v", v=HD), ALU.add)
                    m.then_inc(S["y_sum"].sem, 1)
                    mm_("y_sum", t + 1)
                if t >= 2:
                    mm_("y_dirs", t - 1)
                gn_stats(v_, l, NT + t, Yls[:, t, :].rearrange("p (q r v) -> p q r v", r=2, v=HD))
                gn_squares(v_, l, NT + t)
                if t:
                    finish(t - 1)
            finish(NT - 1)
            for t in range(NT):
                mm_("mixT_mm", t + 1)
                v_.tensor_copy(act[:, 4:8, t * P:(t + 1) * P],
                               PS[:, 5 + 2 * (t % 2), :].rearrange("p (k t) -> p k t", k=4)).then_inc(S["mixT_b"].sem, 1)
            mm_("mixT_a", 5)
            mm_("mixT_b", 5)
            mm_("mix_stored", 64)

        def rwkv_gpsimd(po, l):
            until(po, l, "mu_cols", 4)
            until(po, l, "rwkv_tables", 16 * 11)

            def prep(c):
                cols = slice(rw_col(c), rw_col(c) + P)
                until(po, l, "a_sig", c + 1)
                if c:
                    for d in range(2):
                        until(po, l, f"lk_mm{d}", c)
                    until(po, l, "tok_T", c)
                for ft in range(2):
                    m = po.tensor_scalar(kd[:, :, ft, :], ab[:, :, ft, :], mcol[:, C_V5 + ft:C_V5 + ft + 1],
                                         sml[:, 32 + ft:33 + ft], ALU.mult, ALU.add)
                m.then_inc(S["kd_a"].sem, 1)
                until(po, l, "kd_a", c + 1)
                until(po, l, "shifted", 9)
                po.tensor_tensor(kd[:], kd[:], rwz[:, RW_K:RW_K + 2, cols].unsqueeze(1).broadcast_to([P, 2, 2, P]),
                                 ALU.mult).then_inc(S["kd"].sem, 1)
                until(po, l, "kd", c + 1)
                po.tensor_tensor(rk[:], kd[:, 0, :, :], kd[:, 1, :, :], ALU.add).then_inc(S["kd_sum"].sem, 1)

            def prep_kappa(c):
                until(po, l, "p_inv", c + 1)
                until(po, l, "kd_sum", c + 1)
                po.tensor_tensor(kd[:], kd[:], Pinv[:], ALU.mult).then_inc(S["kappa"].sem, 1)

            prep(0)
            prep_kappa(0)
            for c in range(NT):
                for lv in range(7):
                    for d in range(2):
                        if lv == 0:
                            until(po, l, f"lb{d}", c + 1)
                            if c:
                                until(po, l, f"t1_mm{d}", 6 * c)
                        elif lv == 1:
                            until(po, l, f"lm_T{d}", c + 1)
                            until(po, l, f"xt{d}", 7 * c + 1)
                        else:
                            until(po, l, f"t1_mm{d}", 6 * c + lv - 1)
                        po.tensor_tensor(LM[d][:], LB[d][:, :, 0, :],
                                         lvl[:, d, lv, :].unsqueeze(1).broadcast_to([P, NH, P]), ALU.mult)\
                            .then_inc(S[f"lm{d}"].sem, 1)
                    if lv == 3 and c + 1 < NT:
                        prep(c + 1)
                    if lv == 5 and c + 1 < NT:
                        prep_kappa(c + 1)
            for t in range(NT):
                gn_pool(po, l, NT + t, RWKV_EPS)

        def mod_sum(dve, z, M, w):
            if not (isinstance(M, int) and M == 0):
                dve.wait_ge(s_mm, M)
            for k in range(KD):
                if k == 0:
                    a = dve.tensor_scalar(macc[:, z, :], w[:, k, :], csil[:, k, z:z + 1], None, ALU.mult)
                else:
                    dve.wait_ge(s_ma[z], KD * M + k)
                    a = dve.scalar_tensor_tensor(out=macc[:, z, :], in0=w[:, k, :], scalar=csil[:, k, z:z + 1],
                                                 in1=macc[:, z, :], op0=ALU.mult, op1=ALU.add)
                a.then_inc(s_ma[z], 1)

        block = ctx.enter_context(nc.Block())

        @block.sync
        def _(sp):
            for dst, src in ((csil, i["ccol"]), (ident, i["ident"]), (bmod, i["bmod"]), (ngc, i["ngc"])):
                sp.dma_start(dst[:], src).then_inc(s_const, 16)
            for n in range(MOD_FIRST):
                sp.dma_start(wm0[n][:], i["wm"][n]).then_inc(s_w0[n], 16)
            sp.dma_start(x[:], i["x"]).then_inc(s_x0, 16)

            def load_wi(n, src, unit, j):
                U = u0(n) + unit
                if not (isinstance(unit, int) and U < 2):
                    sp.wait_ge(s_wil, U - 1)
                sp.dma_start(wi[:, j, :, :].rearrange("p k n -> p (k n)"),
                             src[bass.ds(unit, 1)].rearrange("a p n -> p (a n)")).then_inc(s_wi[j], 16)

            def load_wm(M):
                for z in range(2):
                    sp.wait_ge(s_ma[z], KD * M)
                sp.dma_start(wm[:, :, :].rearrange("p k n -> p (k n)"),
                             i["wm"][bass.ds(M, 1)].rearrange("a p k n -> p (a k n)")).then_inc(s_wm, 16)

            def load_wo(n, src, half, unit, slot):
                V = v0(n) + half * OUT_UNITS[SUBS[n % 3]] + unit
                if not (isinstance(unit, int) and V < 2):
                    sp.wait_ge(s_ol, 2 * V - 3)
                sp.dma_start(wo[:, slot, :, :].rearrange("p k n -> p (k n)"),
                             src[half][bass.ds(unit, 1)].rearrange("a p n -> p (a n)")).then_inc(s_wo[slot], 16)

            for n in SUBN:
                l, s = divmod(n, 3)
                if n:
                    sp.wait_ge(s_gm, 4 * n)
                if SUBS[s] == "ffn":
                    src = i["wi"][2 * l + s // 2]
                    M0 = m0(n)
                    for a, b, mod in ffn_parts(n):
                        def step(q):
                            load_wi(n, src, 2 * q, 0)
                            load_wi(n, src, 2 * q + 1, 1)
                            if mod:
                                if isinstance(q, int) and q == 0 and n:
                                    sp.wait_ge(s_om, v0(n))
                                load_wm(M0 + q)
                        over(sp, a, b, step)
                    osrc = i["wo"][2 * l + s // 2]
                    if n == 0:
                        sp.wait_ge(s_ma[1], KD * MOD_FIRST)
                else:
                    sp.dma_start(mcol[:], i["mcol"][l]).then_inc(S["mix_columns"].sem, 16)
                    for q in range(UNITS["mix"]):
                        load_wi(n, i["win"][l], q, q % 2)
                    mix_sync(sp, l)
                    osrc = i["wout"][l]
                nu = OUT_UNITS[SUBS[s]]
                for half in range(2):
                    first = (v0(n) + half * nu) % 2
                    load_wo(n, osrc, half, 0, first)

                    def pair(q):
                        load_wo(n, osrc, half, 2 * q + 1, 1 - first)
                        load_wo(n, osrc, half, 2 * q + 2, first)
                    for a, b in pair_runs(n, half):
                        over(sp, a, b, pair)
                    if nu % 2 == 0:
                        load_wo(n, osrc, half, nu - 1, 1 - first)
            for t in range(NT):
                sp.wait_ge(s_x, 5 * (3 * DEPTH - 1) + t + 1)
                dst = o["y_sample"][t * P:(t + 1) * P, :] if t < NL else o["y_prompt"]
                sp.dma_start(dst, x[:, t, :]).then_inc(s_store, 16)
            sp.wait_ge(s_store, 16 * NT)

        @block.tensor
        def _(pe):
            def mod_unit(M):
                if not (isinstance(M, int) and M == 0):
                    pe.wait_ge(s_me, M)
                for z in range(2):
                    pe.wait_ge(s_ma[z], KD * M + KD)
                    for m in range(MOD_UNIT):
                        mm = pe.matmul(PS[:, 7, 2 * m + z:2 * m + z + 1], macc[:, z, m * P:(m + 1) * P], ones[:, 0:1],
                                       start=True, stop=True)
                mm.then_inc(s_mm, 1)

            pe.wait_ge(s_one, 1)
            for M in range(MOD_FIRST):
                mod_unit(M)

            def transposes(n):
                if n:
                    pe.wait_ge(s_ysq, 10 * n)
                for t in range(NT):
                    pe.wait_ge(s_xn, 5 * n + t + 1)
                    if t >= 2:
                        pe.wait_ge(s_hA, 5 * n + t - 1)
                        pe.wait_ge(s_hD, 5 * n + t - 1)
                    for k in range(KD):
                        mm = pe.transpose(PS[:, 2 * (t % 2) + k // 4, (k % 4) * P:(k % 4 + 1) * P],
                                          xn[:, t % 2, k * P:(k + 1) * P], ident[:])
                    mm.then_inc(s_xT, 1)

            def feature_tile(j, c, cols=P):
                parts = ((0, 384, 128), (384, TOK, 512)) if c == 0 else ((0, 256, 768), (256, TOK, 1024))
                for k in range(KD):
                    for q, (w, h) in enumerate(((wi_hi, h_hi), (wi_hi, h_lo), (wi_lo, h_hi))):
                        st = w[:, j, k, c * P:c * P + cols]
                        for t0, t1, at in parts:
                            at += 3 * j * 512
                            mm = pe.matmul(PSF[0:cols, at:at + t1 - t0], st, h[:, k, t0:t1],
                                           start=(k == 0 and q == 0), stop=(k == KD - 1 and q == 2))
                return mm

            def token_unit(j):
                for t in range(NT):
                    for k in range(KD):
                        for q, (h, w) in enumerate(((h_hi, wi_hi), (h_hi, wi_lo), (h_lo, wi_hi))):
                            mm = pe.matmul(PS[:, 3 * j + t // 2, (t % 2) * 256:(t % 2 + 1) * 256],
                                           h[:, k, t * P:(t + 1) * P], w[:, j, k, :],
                                           start=(k == 0 and q == 0), stop=(k == KD - 1 and q == 2))
                return mm

            def unit_ready(U, first):
                pe.wait_ge(s_wil, U + 1)
                if not first:
                    pe.wait_ge(s_eb, U - 1)

            def gate_rows(n):
                for g in range(4):
                    pe.wait_ge(s_g, 4 * n + g + 1)
                    if 4 * n + g >= 2:
                        pe.wait_ge(s_ge, 4 * n + g - 1)
                    pe.matmul(PS[:, 5 + g % 2, :], ones[:], diag[:, g % 2, :, :], start=True, stop=True)\
                        .then_inc(s_gm, 1)

            def out_unit(n, half, unit, slot):
                V = v0(n) + half * OUT_UNITS[SUBS[n % 3]] + unit
                first = isinstance(unit, int) and unit == 0
                pe.wait_ge(s_ol, 2 * V + 2)
                if first and half:
                    pe.wait_ge(s_ge, 4 * n + 4)
                for kk in range(2):
                    for t in range(NT):
                        bank = (t + 5 * half) % 8
                        if first and half and kk == 0 and bank < 2:
                            pe.wait_ge(s_ysq, 10 * n + bank + 1)
                        for q, (a, w) in enumerate(((a_hi, wo_hi), (a_hi, wo_lo), (a_lo, wo_hi))):
                            start = first and kk == 0 and q == 0
                            mm = pe.matmul(PS[:, bank, :], a[:, slot, kk, t * P:(t + 1) * P], w[:, slot, kk, :],
                                           start=start, stop=True, skip_group_check=True)
                mm.then_inc(s_om, 1)

            for n in SUBN:
                l, s = divmod(n, 3)
                transposes(n)
                low_part_done(pe, n, NT - 1)
                low_part_done(pe, n, NT - 2)
                if SUBS[s] == "ffn":
                    M0 = m0(n)
                    for a, b, mod in ffn_parts(n):
                        def step(q):
                            for j in range(2):
                                U = u0(n) + 2 * q + j
                                unit_ready(U, isinstance(q, int) and u0(n) + 2 * q < 2)
                                feature_tile(j, 0)
                                feature_tile(j, 1).then_inc(s_in, 1)
                            if mod:
                                mod_unit(M0 + q)
                        over(pe, a, b, step)
                else:
                    for q in range(UNITS["mix"]):
                        U = u0(n) + q
                        unit_ready(U, False)
                        if q < 9:
                            if q == 8:
                                mm = feature_tile(q % 2, 0)
                            else:
                                feature_tile(q % 2, 0)
                                mm = feature_tile(q % 2, 1, 64 if q == 1 else P)
                        else:
                            mm = token_unit(q % 2)
                        mm.then_inc(s_in, 1)
                    mix_tensor(pe, l)
                nu = OUT_UNITS[SUBS[s]]
                for half in range(2):
                    first = (v0(n) + half * nu) % 2
                    if half:
                        gate_rows(n)
                    out_unit(n, half, 0, first)

                    def pair(q):
                        out_unit(n, half, 2 * q + 1, 1 - first)
                        out_unit(n, half, 2 * q + 2, first)
                    for a, b in pair_runs(n, half):
                        over(pe, a, b, pair)
                    if nu % 2 == 0:
                        out_unit(n, half, nu - 1, 1 - first)

        @block.scalar
        def _(act_):
            act_.wait_ge(s_const, 16 * 4)
            act_.activation(csil[:], csil[:], ACT.Silu).then_inc(s_c, 1)
            act_.wait_ge(s_c, 1)
            for M in range(MOD_FIRST):
                act_.wait_ge(s_w0[M], 16)
                for k in range(KD):
                    if k == 0:
                        if M:
                            act_.wait_ge(s_mm, M)
                    elif M or k > 2:
                        act_.wait_ge(s_ma[1], KD * M + max(0, k - 2))
                    dst = mprod[:, k % 2, :] if k else macc[:, 1, :]
                    act_.activation(dst, wm0[M][:, k, :], ACT.Copy, scale=csil[:, k, 1:2]).then_inc(s_mp, 1)

            def square_x(n, t):
                if n:
                    act_.wait_ge(s_x, 5 * (n - 1) + t + 1)
                if t:
                    act_.wait_ge(s_sq, 5 * n + t)
                act_.activation(junk[:], x[:, t, :], ACT.Square, accum_out=stat[:, 0, t:t + 1]).then_inc(s_sq, 1)

            def h_lower(n, t):
                act_.wait_ge(s_xT, 5 * n + t + 1)
                if t >= 2:
                    low_part_done(act_, n, t - 2)
                z = 0 if t < NL else 1
                shift = (NMOD * (n // 3) + 3 * (n % 3)) * KD
                for k in range(4):
                    a = act_.activation(h32[:, t % 2, k, :], PS[:, 2 * (t % 2), k * P:(k + 1) * P], ACT.Identity,
                                        bias=modc[:, shift + k, z:z + 1], scale=affA[:, k, z:z + 1])
                a.then_inc(s_hA, 1)
                act_.wait_ge(s_hA, 5 * n + t + 1)
                act_.wait_ge(s_hD, 5 * n + t + 1)
                act_.activation(h_hi[:, :, t * P:(t + 1) * P], h32[:, t % 2, :, :], ACT.Copy).then_inc(s_hhi, 1)

            def cut_wi(n, q, j):
                U = u0(n) + q
                act_.wait_ge(s_wi[j], 16 * (u0(n) // 2 + 1) + (8 * (q - j)))
                if not (isinstance(q, int) and U < 2):
                    act_.wait_ge(s_in, U - 1)
                act_.activation(wi_hi[:, j, :, :], wi[:, j, :, :], ACT.Copy).then_inc(s_wih, 1)

            def silu(U, j, first=False):
                act_.wait_ge(s_in, U + 1)
                if not first:
                    act_.wait_ge(s_eb, U - 1)
                act_.activation(sg[:, j, :], PSF[:, 3 * j * 512 + P:3 * j * 512 + P + TOK], ACT.Silu).then_inc(s_ea, 1)

            def cut_out(n, half, unit, slot):
                V = v0(n) + half * OUT_UNITS[SUBS[n % 3]] + unit
                act_.wait_ge(s_wo[slot], 8 * (V - slot) + 16)
                if not (isinstance(unit, int) and V < 2):
                    act_.wait_ge(s_om, V - 1)
                act_.activation(wo_hi[:, slot, :, :], wo[:, slot, :, :], ACT.Copy).then_inc(s_oh, 1)
                act_.activation(a_hi[:, slot, :, :], act[:, bass.ds(2 * unit, 2), :], ACT.Copy).then_inc(s_oh, 1)

            def square_y(n, half):
                for t in range(NT):
                    act_.wait_ge(s_y, 10 * n + 5 * half + t + 1)
                    bank = PS[:, (t + 5 * half) % 8, :]
                    act_.activation(bank, bank, ACT.Square, accum_out=stat[:, 2 + 2 * half, t:t + 1]).then_inc(s_ysq, 1)

            def gate_rows_out(n):
                for g in range(4):
                    z, half = divmod(g, 2)
                    act_.wait_ge(s_gm, 4 * n + g + 1)
                    if n and g == 0:
                        act_.wait_ge(s_y, 10 * n)
                    act_.activation(gates[:, z, half * 512:(half + 1) * 512], PS[:, 5 + g % 2, :], ACT.Copy)\
                        .then_inc(s_ge, 1)

            for n in SUBN:
                l, s = divmod(n, 3)
                if n == 0:
                    act_.wait_ge(s_x0, 16)
                    act_.wait_ge(s_mm, MOD_FIRST)
                for t in range(NT):
                    square_x(n, t)
                if n == 0:
                    for q in range(2):
                        cut_wi(n, q, q)
                act_.wait_ge(s_aff, n + 1)
                for t in range(NT):
                    h_lower(n, t)
                if SUBS[s] == "ffn":
                    def step(q):
                        first = isinstance(q, int) and q == 0
                        U = u0(n) + 2 * q
                        if not first:
                            cut_wi(n, 2 * q, 0)
                            silu(U - 1, 1, isinstance(q, int) and U == 2)
                            cut_wi(n, 2 * q + 1, 1)
                        silu(U, 0, first and n == 0)
                    for a, b in ((0, 1), (1, 2), (2, NF // 2)) if n == 0 else ((0, 1), (1, NF // 2)):
                        over(act_, a, b, step)
                    silu(u0(n) + NF - 1, 1)
                    act_.wait_ge(s_eb, u0(n) + NF)
                else:
                    for q in range(UNITS["mix"] + 1):
                        if 2 <= q < UNITS["mix"]:
                            cut_wi(n, q, q % 2)
                        if q:
                            first_half_out(act_, l, q - 1)
                        for f in SHIFT_AT.get(q, ()):
                            shift_scalar(act_, l, f)
                    mix_scalar(act_, l)
                nu = OUT_UNITS[SUBS[s]]
                for half in range(2):
                    first = (v0(n) + half * nu) % 2
                    cut_out(n, half, 0, first)
                    if half:
                        gate_rows_out(n)
                        square_y(n, 0)

                    def pair(q):
                        cut_out(n, half, 2 * q + 1, 1 - first)
                        cut_out(n, half, 2 * q + 2, first)
                    for a, b in pair_runs(n, half):
                        over(act_, a, b, pair)
                    if nu % 2 == 0:
                        cut_out(n, half, nu - 1, 1 - first)
                if n + 1 < len(SUBN):
                    for q in range(2):
                        cut_wi(n + 1, q, q)
                square_y(n, 1)

        @block.vector
        def _(dve):
            dve.memset(ones[:], 1.0).then_inc(s_one, 1)

            def mod_out(M):
                dve.wait_ge(s_mm, M + 1)
                dve.tensor_tensor(modc[:, bass.ds(MOD_UNIT * M, MOD_UNIT), :],
                                  PS[:, 7, 0:2 * MOD_UNIT].rearrange("p (m z) -> p m z", z=2),
                                  bmod[:, bass.ds(MOD_UNIT * M, MOD_UNIT)].unsqueeze(2)
                                  .broadcast_to([P, MOD_UNIT, 2]), ALU.add).then_inc(s_me, 1)

            dve.wait_ge(s_const, 16 * 4)
            dve.wait_ge(s_c, 1)
            for M in range(MOD_FIRST):
                dve.wait_ge(s_w0[M], 16)
                mod_sum(dve, 0, M, wm0[M])
                mod_out(M)

            def columns(n):
                at = (NMOD * (n // 3) + 3 * (n % 3)) * KD
                dve.wait_ge(s_me, m0(n))
                dve.scalar_tensor_tensor(
                    out=affA[:], in0=modc[:, at + KD:at + 2 * KD, :], scalar=1.0,
                    in1=ngc[:, 6 * (n // 3) + 2 * (n % 3), :].unsqueeze(2).broadcast_to([P, KD, 2]),
                    op0=ALU.add, op1=ALU.mult).then_inc(s_aff, 1)

            def norm_x(n, t):
                dve.wait_ge(s_rs, 5 * n + t + 1)
                if t >= 2:
                    dve.wait_ge(s_xT, 5 * n + t - 1)
                dve.tensor_scalar(xn[:, t % 2, :], x[:, t, :], stat[:, 1, t:t + 1], None, ALU.mult).then_inc(s_xn, 1)

            def h_upper(n, t):
                dve.wait_ge(s_xT, 5 * n + t + 1)
                if t >= 2:
                    low_part_done(dve, n, t - 2)
                z = 0 if t < NL else 1
                shift = (NMOD * (n // 3) + 3 * (n % 3)) * KD
                for k in range(4, KD):
                    a = dve.tensor_scalar(h32[:, t % 2, k, :], PS[:, 2 * (t % 2) + 1, (k - 4) * P:(k - 3) * P],
                                          affA[:, k, z:z + 1], modc[:, shift + k, z:z + 1], ALU.mult, ALU.add)
                a.then_inc(s_hD, 1)

            def h_low_part(n, t):
                if t % 2:
                    return
                dve.wait_ge(s_hhi, 5 * n + t + 1)
                dve.tensor_tensor(h_lo[:, :, t * P:(t + 1) * P], h32[:, t % 2, :, :],
                                  h_hi[:, :, t * P:(t + 1) * P].bitcast(F32), ALU.subtract).then_inc(s_hlo, 1)

            def cut_wi(U, j):
                dve.wait_ge(s_wih, U + 1)
                dve.tensor_tensor(wi_lo[:, j, :, :], wi[:, j, :, :], wi_hi[:, j, :, :].bitcast(F32),
                                  ALU.subtract).then_inc(s_wil, 1)

            def hidden(n, f, j):
                dve.wait_ge(s_ea, u0(n) + f + 1)
                up = (3 * j + 1) * 512 + 256
                dve.tensor_tensor(tile_at(act, f), sg[:, j, :], PSF[:, up:up + TOK], ALU.mult).then_inc(s_eb, 1)

            def cut_out(n, half, unit, slot):
                V = v0(n) + half * OUT_UNITS[SUBS[n % 3]] + unit
                dve.wait_ge(s_oh, 2 * V + 1)
                dve.tensor_tensor(wo_lo[:, slot, :, :], wo[:, slot, :, :], wo_hi[:, slot, :, :].bitcast(F32),
                                  ALU.subtract).then_inc(s_ol, 1)
                dve.wait_ge(s_oh, 2 * V + 2)
                dve.tensor_tensor(a_lo[:, slot, :, :], act[:, bass.ds(2 * unit, 2), :],
                                  a_hi[:, slot, :, :].bitcast(F32), ALU.subtract).then_inc(s_ol, 1)

            def y_out(n, half):
                dve.wait_ge(s_om, v0(n) + (half + 1) * OUT_UNITS[SUBS[n % 3]])
                dve.wait_ge(s_ge, 4 * n + 4)
                for t in range(NT):
                    at = slice(half * 512, (half + 1) * 512)
                    dve.tensor_tensor(y[:, t, at], PS[:, (t + 5 * half) % 8, :], gates[:, 0 if t < NL else 1, at],
                                      ALU.mult).then_inc(s_y, 1)

            for n in SUBN:
                l, s = divmod(n, 3)
                columns(n)
                if n == 0:
                    for q in range(2):
                        cut_wi(q, q)
                norm_x(n, 0)
                for t in range(NT):
                    if t + 1 < NT:
                        norm_x(n, t + 1)
                    h_upper(n, t)
                    h_low_part(n, t)
                if SUBS[s] == "ffn":
                    M0 = m0(n)
                    for a, b, mod in ffn_parts(n):
                        def step(q):
                            first = isinstance(q, int) and q == 0
                            U = u0(n) + 2 * q
                            if not first:
                                cut_wi(U, 0)
                                hidden(n, 2 * q - 1, 1)
                                cut_wi(U + 1, 1)
                            if not first and (mod or isinstance(q, int)):
                                mod_out(M0 + q - 1)
                            if mod:
                                dve.wait_ge(s_wm, 16 * (M0 + q - MOD_FIRST) + 16)
                                mod_sum(dve, 0, M0 + q, wm)
                            hidden(n, 2 * q, 0)
                            if mod:
                                mod_sum(dve, 1, M0 + q, wm)
                        over(dve, a, b, step)
                    hidden(n, NF - 1, 1)
                    dve.wait_ge(s_eb, u0(n) + NF)
                else:
                    for q in range(UNITS["mix"] + 1):
                        if 2 <= q < UNITS["mix"]:
                            cut_wi(u0(n) + q, q % 2)
                        if q:
                            second_half_out(dve, l, q - 1)
                        for f in SHIFT_AT.get(q, ()):
                            shift_vector(dve, l, f)
                    mix_vector(dve, l)
                nu = OUT_UNITS[SUBS[s]]
                for half in range(2):
                    first = (v0(n) + half * nu) % 2
                    cut_out(n, half, 0, first)
                    if half:
                        y_out(n, 0)

                    def pair(q):
                        cut_out(n, half, 2 * q + 1, 1 - first)
                        cut_out(n, half, 2 * q + 2, first)
                    for a, b in pair_runs(n, half):
                        over(dve, a, b, pair)
                    if nu % 2 == 0:
                        cut_out(n, half, nu - 1, 1 - first)
                if n + 1 < len(SUBN):
                    for q in range(2):
                        cut_wi(u0(n + 1) + q, q)
                y_out(n, 1)
                for t in range(NT):
                    dve.wait_ge(s_yrs, 5 * n + t + 1)
                    dve.wait_ge(s_y, 10 * n + 6 + t)
                    dve.scalar_tensor_tensor(out=x[:, t, :], in0=y[:, t, :], scalar=stat[:, 3, t:t + 1],
                                             in1=x[:, t, :], op0=ALU.mult, op1=ALU.add).then_inc(s_x, 1)

        @block.gpsimd
        def _(pool):
            pool.memset(powe[:], -0.5).then_inc(s_one, 1)
            pool.wait_ge(s_one, 2)

            def rstd(src, dst, t, done, ms, count):
                pool.tensor_scalar(stat[:, src, t:t + 1], stat[:, src, t:t + 1], 1.0 / D, NORM_EPS, ALU.mult,
                                   ALU.add).then_inc(ms, 1)
                pool.wait_ge(ms, count)
                pool.tensor_tensor(stat[:, dst, t:t + 1], stat[:, src, t:t + 1], powe[:, 0:1],
                                   ALU.pow).then_inc(done, 1)

            def h_low_part(n, t):
                pool.wait_ge(s_hhi, 5 * n + t + 1)
                pool.tensor_tensor(h_lo[:, :, t * P:(t + 1) * P], h32[:, t % 2, :, :],
                                   h_hi[:, :, t * P:(t + 1) * P].bitcast(F32), ALU.subtract).then_inc(s_hlp, 1)

            def gate_diagonals(n):
                at = (NMOD * (n // 3) + 3 * (n % 3) + 2) * KD
                pool.wait_ge(s_me, (at + KD) // MOD_UNIT)
                if n:
                    pool.wait_ge(s_g, 4 * n)
                pool.tensor_tensor(gcol[:], modc[:, at:at + KD, :],
                                   ngc[:, 6 * (n // 3) + 2 * (n % 3) + 1, :].unsqueeze(2).broadcast_to([P, KD, 2]),
                                   ALU.mult).then_inc(s_gc, 1)
                pool.wait_ge(s_gc, 2 * n + 1)
                pool.tensor_scalar(gcol[:], gcol[:], 0.5 if SUBS[n % 3] == "ffn" else 1.0, None, ALU.mult)\
                    .then_inc(s_gc, 1)
                pool.wait_ge(s_gc, 2 * n + 2)
                for g in range(4):
                    z, half = divmod(g, 2)
                    if g >= 2:
                        pool.wait_ge(s_gm, 4 * n + g - 1)
                    for k in range(4):
                        a = pool.tensor_scalar(diag[:, g % 2, k, :], ident[:], gcol[:, 4 * half + k, z:z + 1], None,
                                               ALU.mult)
                    a.then_inc(s_g, 1)

            pool.wait_ge(s_c, 1)
            def mod_add(M, k):
                pool.wait_ge(s_mp, KD * M + k + 1)
                if k >= 2:
                    pool.wait_ge(s_ma[1], KD * M + k - 1)
                pool.tensor_tensor(macc[:, 1, :], macc[:, 1, :], mprod[:, k % 2, :], ALU.add)\
                    .then_inc(s_ma[1], 2 if k == KD - 1 else 1)

            for M in range(MOD_FIRST):
                for k in range(1, KD):
                    mod_add(M, k)
            for n in SUBN:
                for t in range(NT):
                    pool.wait_ge(s_sq, 5 * n + t + 1)
                    rstd(0, 1, t, s_rs, s_rms, 5 * n + t + 1)
                h_low_part(n, 1)
                h_low_part(n, 3)
                if SUBS[n % 3] == "mix":
                    shift_gpsimd(pool, n // 3)
                if SUBS[n % 3] == "ffn":
                    pool.wait_ge(s_eb, u0(n) + NF)
                else:
                    mix_gpsimd(pool, n // 3)
                    until(pool, n // 3, "rwkv_o", NT)
                gate_diagonals(n)
                for t in range(NT):
                    pool.wait_ge(s_ysq, 10 * n + 5 + t + 1)
                    pool.tensor_tensor(stat[:, 2, t:t + 1], stat[:, 2, t:t + 1], stat[:, 4, t:t + 1], ALU.add)\
                        .then_inc(s_yms, 1)
                    pool.wait_ge(s_yms, 2 * (5 * n + t) + 1)
                    rstd(2, 3, t, s_yrs, s_yms, 2 * (5 * n + t + 1))


def mix_layouts(a, r):
    f = np.float32
    c = np.ascontiguousarray
    wi = a["w_in"]
    off = {"qa": 0, "kva": 256, "kr": 384, "r": 416, "k": 672, "v": 928, "zw": 1184, "za": 1312, "zg": 1440,
           "rq": 1568, "rk": 1824, "rv": 2080, "gf": 2336, "gb": 2592}
    col = lambda n, w: wi[:, :, off[n]:off[n] + w]
    zero = lambda w: np.zeros((DEPTH, D, w), f)

    def swap(d):
        j = np.arange(2 * d)
        return np.where(j % d < d // 2, j + d // 2, j - d // 2)

    units = [col("qa", 256), np.concatenate([col("kva", 128), col("kr", 32), col("kr", 32)[:, :, swap(16)], zero(64)], 2),
             col("r", 256), col("k", 256), col("v", 256), col("zw", 256), col("rq", 256), col("rk", 256),
             np.concatenate([col("zg", 128), zero(128)], 2), col("gf", 256), col("gb", 256), col("rv", 256)]
    r["win"] = c(np.stack(units, 1).reshape(DEPTH, 12, KD, P, 256).transpose(0, 1, 3, 2, 4).reshape(DEPTH, 12, P, -1))
    wo = a["w_out"].reshape(DEPTH, KD // 2, 2, P, 2, 512)
    r["wout"] = c(wo.transpose(0, 4, 1, 3, 2, 5).reshape(DEPTH, 2, KD // 2, P, 1024))

    def rope(width):
        d = width // 2
        t = np.arange(LAT)
        inv = 10000.0 ** (-np.arange(d // 2) / (d // 2))
        cos, sin = np.ones((width, TOK)), np.zeros((width, TOK))
        for b, pos in enumerate((t // 64, t % 64)):
            ang = inv[:, None] * pos[None, :]
            for s, sign in ((0, -1.0), (1, 1.0)):
                at = b * d + s * (d // 2)
                cos[at:at + d // 2, :LAT] = np.cos(ang)
                sin[at:at + d // 2, :LAT] = sign * np.sin(ang)
        return [c(np.tile(v, (P // width, 1)).astype(f)) for v in (cos, sin)]
    r["cosm"], r["sinm"] = rope(ROPE)
    r["cosr"], r["sinr"] = rope(HD)
    perm = np.concatenate([swap(32), 64 + swap(32)])
    pt = np.zeros((P, P), f)
    pt[perm, np.arange(P)] = 1.0
    r["permT"] = pt
    wq = a["mla_wq_up"].reshape(DEPTH, QL, H_MLA, NOPE + ROPE)
    wq = np.concatenate([wq, wq[..., NOPE:][..., swap(16)]], -1)
    r["wq"] = c(wq.reshape(DEPTH, 2, P, H_MLA * P).transpose(0, 2, 1, 3))
    kv = a["mla_wkv_up"].reshape(DEPTH, KVL, H_MLA, NOPE + VHD)
    r["wk"] = c(kv[..., :NOPE].reshape(DEPTH, KVL, 512))
    r["wv"] = c(kv[..., NOPE:].reshape(DEPTH, KVL, 512))
    r["ckvc"] = c(a["cache_mla_ckv"][0].transpose(0, 2, 1))
    r["krc"] = c(a["cache_mla_krope"][0].transpose(0, 2, 1))
    vec = a["rwkv_vec"]
    tiles = lambda v: v.reshape(DEPTH, -1, P).transpose(0, 2, 1)
    r["mcol"] = c(np.concatenate([tiles(a["mla_norm_q"]), tiles(a["mla_norm_kv"]), tiles(a["rwkv_mu"]),
                                  tiles(vec[:, 4]), tiles(vec[:, 5]), tiles(vec[:, 6]), tiles(vec[:, 2]),
                                  tiles(vec[:, 3])], 2))
    n = np.arange(P)
    g = np.array([[1.0 - 2.0 ** -(5 + h + 0.5 * d) for d in range(2)] for h in range(NH)])
    dm = np.zeros((P, NH, 2, P))
    diff = n[None, :] - n[:, None]
    xi = np.zeros((P, 2, 2, P))
    zeta = np.zeros((P, NH, 2))
    gch = np.zeros((P, 2, 2))
    for h in range(NH):
        ft, rws = h // 2, slice((h % 2) * HD, (h % 2 + 1) * HD)
        for d in range(2):
            s = diff if d == 0 else -diff
            dm[:, h, d, :] = np.where(s >= 0, g[h, d] ** np.maximum(s, 0), 0.0) / 8
            xi[rws, d, ft, :] = g[h, d] ** (n + 1 if d == 0 else P - n)
            zeta[:, h, d] = g[h, d] ** (P - 1 - n if d == 0 else n) / 8
            gch[rws, d, ft] = g[h, d] ** P
    r["dmask"], r["xi"], r["zeta"], r["gch"] = (c(v.astype(f)) for v in (dm, xi, zeta, gch))
    row = lambda v: c(np.broadcast_to(v[:, None, :], (DEPTH, P, v.shape[-1])))
    r["rgn"] = row(a["ret_gn"].reshape(DEPTH, 512))

    def state(v):
        v = v[0].reshape(DEPTH, 2, 2, 2, HD, HD)
        return c(v.transpose(0, 3, 4, 1, 2, 5).reshape(DEPTH, P, 2, 2, HD))
    r["st_ret"] = state(a["state_ret"])
    r["st_rwkv"] = state(a["state_rwkv"].swapaxes(-1, -2))
    u, t = n[:, None], n[None, :]
    tri = np.stack([np.concatenate([u < t, u <= t], 1), np.concatenate([u > t, u >= t], 1)], 1)
    r["tri"] = c((tri * -DECAY_SCALE).astype(f))
    r["mask2"] = c(np.stack([np.stack([u < t, u <= t], 1), np.stack([u > t, u >= t], 1)], 1).astype(f))
    lvl = np.zeros((P, 2, 7, P), f)
    for k in range(7):
        b = 2 ** k
        same, su, st = u // (2 * b) == t // (2 * b), (u // b) % 2, (t // b) % 2
        lvl[:, 0, k, :] = same & (su == 0) & (st == 1)
        lvl[:, 1, k, :] = same & (su == 1) & (st == 0)
    r["lvl"] = lvl
    r["blk"] = c((u // HD == t // HD).astype(f))
    r["hsel"] = c((u // HD == np.arange(2)[None, :]).astype(f))
    r["id64"] = c((u % HD == np.arange(HD)[None, :]).astype(f))
    up = a["rwkv_lora_up"]
    r["upw"] = c(up[:, 0:2].reshape(DEPTH, P, DR))
    r["upa"] = c(up[:, 2:4].reshape(DEPTH, P, DR))
    r["gup"] = c(a["rwkv_g_up"])
    r["v7"] = row(vec[:, 7])
    r["v01"] = row(vec[:, 0:2].reshape(DEPTH, 512))


def layouts(a):
    f = np.float32
    c = np.ascontiguousarray
    r = {}
    r["ccol"] = c(np.stack([a["c"][0], a["c_ctx"]], -1).reshape(KD, P, 2).transpose(1, 0, 2))
    r["ident"] = np.eye(P, dtype=f)
    r["bmod"] = c(a["b_mod"].reshape(DEPTH * NMOD * KD, P).T)
    r["ngc"] = c(a["norm_g"].reshape(DEPTH * 6, KD, P).transpose(2, 0, 1))
    r["wm"] = c(a["w_mod"].reshape(DEPTH, KD, P, NMOD * KD // MOD_UNIT, MOD_UNIT * P)
                .transpose(0, 3, 2, 1, 4).reshape(MOD_UNITS, P, KD, MOD_UNIT * P))
    xs = np.concatenate([a["x_sample"][0], a["x_prompt"][0]], 0)
    r["x"] = c(xs.reshape(NT, P, D).transpose(1, 0, 2))
    wi = a["ffn_wi"].reshape(2 * DEPTH, KD, P, 2, NF, P)
    r["wi"] = c(wi.transpose(0, 4, 2, 1, 3, 5).reshape(2 * DEPTH, NF, P, KD * 2 * P))
    wo = a["ffn_wo"].reshape(2 * DEPTH, NF // 2, 2, P, 2, 512)
    r["wo"] = c(wo.transpose(0, 4, 1, 3, 2, 5).reshape(2 * DEPTH, 2, NF // 2, P, 1024))
    mix_layouts(a, r)
    return r


_OUTS = [("y_prompt", (CTX, D)), ("y_sample", (LAT, D)), ("ckv", (DEPTH, P, KVL)), ("krope", (DEPTH, P, ROPE)),
         ("s_rwkv", (DEPTH, P, 2, 2, HD)), ("s_ret", (DEPTH, P, 2, 2, HD))]


def kernel(**inputs):
    import concourse.bacc as _bacc
    from concourse.bass_utils import run_bass_kernel_spmd as _run

    nc = _bacc.Bacc("TRN2", target_bir_lowering=False, num_devices=1)
    arrays = layouts({k: np.asarray(v) for k, v in inputs.items()})
    ins = {k: nc.dram_tensor("in_" + k, v.shape, mybir.dt.from_np(v.dtype), kind="ExternalInput").ap()
           for k, v in arrays.items()}
    outs = {k: nc.dram_tensor("out_" + k, s, F32, kind="ExternalOutput").ap() for k, s in _OUTS}
    build(nc, ins, outs)
    r = _run(nc, [{"in_" + k: v for k, v in arrays.items()}], core_ids=[0]).results[0]
    g = {k: r["out_" + k] for k, _ in _OUTS}
    st = lambda v: v.reshape(DEPTH, 2, HD, 2, 2, HD).transpose(0, 3, 4, 1, 2, 5).reshape(1, DEPTH, 2, NH, HD, HD)
    return (g["y_prompt"][None], g["y_sample"][None], g["ckv"][None], g["krope"][None],
            np.ascontiguousarray(st(g["s_rwkv"]).swapaxes(-1, -2)), np.ascontiguousarray(st(g["s_ret"])))
```
